# Optimizing a Trainium2 kernel written in Bass

```python
import math
import jax
import jax.numpy as jnp
from jax import lax
import numpy as np

D_MODEL = 1024
BATCH = 1
SEQ = 1024
DEPTH = 1
DEC_BATCH = 8
DEC_SEQ = 1
PAST_LEN = 8192
PAGE_SIZE = 128

GLA_HEADS = 4
GLA_DV = D_MODEL // GLA_HEADS
GLA_DK = GLA_DV // 2
GLA_GATE_RANK = 16
GLA_TAU = 16.0
GLA_QK = GLA_HEADS * GLA_DK
GLA_V = GLA_HEADS * GLA_DV
ML_HEADS = 4
ML_DH = D_MODEL // ML_HEADS
ML_W = ML_HEADS * ML_DH
CONV_W = 4
CHUNK = 64
PEER_HEADS = 8
PEER_DQ = 256
N_KEYS = 128
N_EXPERTS = N_KEYS * N_KEYS
PEER_TOPK = 16
TOKEN_BLOCK = 256
EPS = 1e-6

SPLITS = (GLA_QK, GLA_QK, GLA_V, GLA_V, GLA_GATE_RANK,
          ML_W, ML_W, ML_W, ML_HEADS, ML_HEADS, ML_W,
          D_MODEL, D_MODEL)
N_IN = (2 * GLA_QK + 2 * GLA_V + GLA_GATE_RANK + 4 * ML_W + 2 * ML_HEADS + 2 * D_MODEL)

kernel_name = "gla_mlstm_peer_hybrid_step"

def _rmsnorm(x, g):
    xf = x.astype(jnp.float32)
    y = xf * lax.rsqrt(jnp.mean(xf * xf, axis=-1, keepdims=True) + EPS)
    return (y * g.astype(jnp.float32)).astype(x.dtype)

def _headnorm(x, g, n_heads):
    shp = x.shape
    xf = x.astype(jnp.float32).reshape(shp[:-1] + (n_heads, shp[-1] // n_heads))
    y = xf * lax.rsqrt(jnp.mean(xf * xf, axis=-1, keepdims=True) + EPS)
    return y.reshape(shp) * g.astype(jnp.float32)

def _chunk_len(t):
    return CHUNK if t % CHUNK == 0 else t

def _to_chunks(x, n, l):
    b = x.shape[0]
    x = x.reshape((b, n, l) + x.shape[2:])
    return jnp.moveaxis(x, [1, 3], [0, 2])

def _from_chunks(o):
    o = jnp.moveaxis(o, [0, 2], [1, 3])
    return o.reshape((o.shape[0], o.shape[1] * o.shape[2]) + o.shape[3:])

def _gla(q, k, v, log_a, s0):
    t = q.shape[1]
    l = _chunk_len(t)
    n = t // l
    f32 = jnp.float32
    qc = _to_chunks(q.astype(f32), n, l)
    kc = _to_chunks(k.astype(f32), n, l)
    vc = _to_chunks(v.astype(f32), n, l)
    ac = _to_chunks(log_a.astype(f32), n, l)
    mask = jnp.tril(jnp.ones((l, l), dtype=bool))

    def step(s, inp):
        qb, kb, vb, ab = inp
        bc = jnp.cumsum(ab, axis=2)
        diff = bc[:, :, :, None, :] - bc[:, :, None, :, :]
        dec = jnp.exp(jnp.where(mask[:, :, None], diff, -jnp.inf))
        att = jnp.einsum('bhld,bhsd,bhlsd->bhls', qb, kb, dec)
        o = (jnp.einsum('bhld,bhdv->bhlv', qb * jnp.exp(bc), s)
             + jnp.einsum('bhls,bhsv->bhlv', att, vb))
        b_last = bc[:, :, -1, :]
        s = (s * jnp.exp(b_last)[..., None]
             + jnp.einsum('bhsd,bhsv->bhdv', kb * jnp.exp(b_last[:, :, None, :] - bc), vb))
        return s, o

    s, o = lax.scan(step, s0.astype(f32), (qc, kc, vc, ac))
    return _from_chunks(o), s

def _mlstm(q, k, v, i_pre, f_pre, c0, n0, m0):
    t = q.shape[1]
    l = _chunk_len(t)
    n = t // l
    f32 = jnp.float32
    qc = _to_chunks(q.astype(f32), n, l)
    kc = _to_chunks(k.astype(f32), n, l)
    vc = _to_chunks(v.astype(f32), n, l)
    lic = _to_chunks(i_pre.astype(f32), n, l)
    lfc = _to_chunks(jax.nn.log_sigmoid(f_pre.astype(f32)), n, l)
    mask = jnp.tril(jnp.ones((l, l), dtype=bool))

    def step(carry, inp):
        c, nv, m = carry
        qb, kb, vb, lib, lfb = inp
        b = jnp.cumsum(lfb, axis=-1)
        a_inter = b + m[..., None]
        dmat = jnp.where(mask, b[..., :, None] - b[..., None, :] + lib[..., None, :], -jnp.inf)
        m_t = jnp.maximum(a_inter, jnp.max(dmat, axis=-1))
        w_inter = jnp.exp(a_inter - m_t)
        s = jnp.einsum('bhld,bhsd->bhls', qb, kb) * jnp.exp(dmat - m_t[..., None])
        num = (w_inter[..., None] * jnp.einsum('bhld,bhdv->bhlv', qb, c)
               + jnp.einsum('bhls,bhsv->bhlv', s, vb))
        den = w_inter * jnp.einsum('bhld,bhd->bhl', qb, nv) + jnp.sum(s, axis=-1)
        h = num / jnp.maximum(jnp.abs(den), jnp.exp(-m_t))[..., None]
        b_last = b[..., -1]
        g_s = b_last[..., None] - b + lib
        m_new = jnp.maximum(b_last + m, jnp.max(g_s, axis=-1))
        f_c = jnp.exp(b_last + m - m_new)
        w_s = jnp.exp(g_s - m_new[..., None])
        c = f_c[..., None, None] * c + jnp.einsum('bhs,bhsd,bhsv->bhdv', w_s, kb, vb)
        nv = f_c[..., None] * nv + jnp.einsum('bhs,bhsd->bhd', w_s, kb)
        return (c, nv, m_new), h

    (c, nv, m), h = lax.scan(step, (c0.astype(f32), n0.astype(f32), m0.astype(f32)),
                             (qc, kc, vc, lic, lfc))
    return _from_chunks(h), c, nv, m

def _causal_conv(x, buf, w, b):
    t = x.shape[1]
    xp = jnp.concatenate([buf.astype(x.dtype), x], axis=1)
    y = b
    for j in range(CONV_W):
        y = y + w[j] * xp[:, j:j + t]
    return y, xp[:, xp.shape[1] - (CONV_W - 1):]

def _mixer(h, s_gla, s_c, s_n, s_m, s_conv, w_in, gla_w2, gla_b2, gla_norm_g,
           conv_w, conv_b, ml_i_b, ml_f_b, ml_norm_g, w_out):
    bsz, t, _ = h.shape
    proj = h @ w_in
    points = np.cumsum(np.array(SPLITS))[:-1].tolist()
    (aq, ak, av, ag, alr, bq, bk, bv, bi, bf, bo, gate_a, gate_b) = jnp.split(proj, points, axis=-1)

    log_a = jax.nn.log_sigmoid((alr @ gla_w2 + gla_b2).astype(jnp.float32)) / GLA_TAU
    q_a = aq.reshape(bsz, t, GLA_HEADS, GLA_DK) * (GLA_DK ** -0.5)
    k_a = ak.reshape(bsz, t, GLA_HEADS, GLA_DK)
    v_a = av.reshape(bsz, t, GLA_HEADS, GLA_DV)
    o_a, s_gla_new = _gla(q_a, k_a, v_a, log_a.reshape(bsz, t, GLA_HEADS, GLA_DK), s_gla)
    o_a = (_headnorm(o_a.reshape(bsz, t, GLA_V), gla_norm_g, GLA_HEADS).astype(h.dtype)
           * jax.nn.silu(ag))

    qk, conv_new = _causal_conv(jnp.concatenate([bq, bk], axis=-1), s_conv, conv_w, conv_b)
    qk = jax.nn.silu(qk)
    q_b, k_b = jnp.split(qk, 2, axis=-1)
    o_b, c_new, n_new, m_new = _mlstm(
        q_b.reshape(bsz, t, ML_HEADS, ML_DH),
        k_b.reshape(bsz, t, ML_HEADS, ML_DH) * (ML_DH ** -0.5),
        bv.reshape(bsz, t, ML_HEADS, ML_DH),
        bi + ml_i_b, bf + ml_f_b, s_c, s_n, s_m)
    o_b = (_headnorm(o_b.reshape(bsz, t, ML_W), ml_norm_g, ML_HEADS).astype(h.dtype)
           * jax.nn.sigmoid(bo))

    mix = (jax.nn.sigmoid(gate_a) * o_a + jax.nn.sigmoid(gate_b) * o_b) @ w_out
    return mix, s_gla_new, c_new, n_new, m_new, conv_new

def _peer(h, wq, subkeys, u_tab, v_tab):
    bsz, t, d = h.shape
    n_tok = bsz * t
    pad = (-n_tok) % TOKEN_BLOCK
    xf = jnp.pad(h.reshape(n_tok, d), ((0, pad), (0, 0)))
    blocks = xf.reshape(-1, TOKEN_BLOCK, d)

    def one(xb):
        q = (xb @ wq).reshape(TOKEN_BLOCK, PEER_HEADS, 2, PEER_DQ // 2)
        s = jnp.einsum('thcd,ckd->thck', q, subkeys)
        sv, si = lax.top_k(s, PEER_TOPK)
        cand = (sv[:, :, 0, :, None] + sv[:, :, 1, None, :]).reshape(TOKEN_BLOCK, PEER_HEADS, -1)
        cidx = (si[:, :, 0, :, None] * N_KEYS + si[:, :, 1, None, :]).reshape(TOKEN_BLOCK, PEER_HEADS, -1)
        top_v, top_pos = lax.top_k(cand, PEER_TOPK)
        eidx = jnp.take_along_axis(cidx, top_pos, axis=-1)
        g = jax.nn.softmax(top_v.astype(jnp.float32), axis=-1).astype(xb.dtype)
        u = u_tab[eidx]
        a = jax.nn.gelu(jnp.einsum('td,thkd->thk', xb, u), approximate=False)
        v = v_tab[eidx]
        return jnp.einsum('thk,thkd->td', g * a, v)

    out = lax.map(one, blocks).reshape(-1, d)[:n_tok]
    return out.reshape(bsz, t, d)

def _trunk(x, st_gla, st_c, st_n, st_m, st_conv,
           norm1_g, w_in, gla_w2, gla_b2, gla_norm_g, conv_w, conv_b, ml_i_b, ml_f_b,
           ml_norm_g, w_out, norm2_g, peer_wq, peer_subkeys, peer_u, peer_v, final_g):
    new_gla, new_c, new_n, new_m, new_conv = [], [], [], [], []
    for li in range(DEPTH):
        h = _rmsnorm(x, norm1_g[li])
        mix, sg, sc, sn, sm, sv = _mixer(
            h, st_gla[li], st_c[li], st_n[li], st_m[li], st_conv[li],
            w_in[li], gla_w2[li], gla_b2[li], gla_norm_g[li], conv_w[li], conv_b[li],
            ml_i_b[li], ml_f_b[li], ml_norm_g[li], w_out[li])
        x = x + mix
        x = x + _peer(_rmsnorm(x, norm2_g[li]), peer_wq[li], peer_subkeys[li], peer_u[li], peer_v[li])
        new_gla.append(sg.astype(x.dtype))
        new_c.append(sc.astype(x.dtype))
        new_n.append(sn.astype(x.dtype))
        new_m.append(sm.astype(x.dtype))
        new_conv.append(sv.astype(x.dtype))
    y = _rmsnorm(x, final_g)
    return (y, jnp.stack(new_gla), jnp.stack(new_c), jnp.stack(new_n),
            jnp.stack(new_m), jnp.stack(new_conv))

def setup_inputs(seed: int = 0) -> dict:
    key = jax.random.key(seed)
    ks = jax.random.split(key, 24)
    nrm = jax.random.normal
    f32 = jnp.float32
    d = D_MODEL
    inp = {}
    inp['x_prompt'] = nrm(ks[0], (BATCH, SEQ, d), f32)
    inp['x_sample'] = nrm(ks[1], (DEC_BATCH, DEC_SEQ, d), f32)
    inp['state_gla'] = 0.3 * nrm(ks[2], (DEPTH, DEC_BATCH, GLA_HEADS, GLA_DK, GLA_DV), f32)
    inp['state_mlstm_c'] = 0.3 * nrm(ks[3], (DEPTH, DEC_BATCH, ML_HEADS, ML_DH, ML_DH), f32)
    inp['state_mlstm_n'] = 0.3 * nrm(ks[4], (DEPTH, DEC_BATCH, ML_HEADS, ML_DH), f32)
    inp['state_mlstm_m'] = nrm(ks[5], (DEPTH, DEC_BATCH, ML_HEADS), f32)
    inp['state_conv'] = nrm(ks[6], (DEPTH, DEC_BATCH, CONV_W - 1, 2 * ML_W), f32)
    inp['norm1_g'] = 1.0 + 0.02 * nrm(ks[7], (DEPTH, d), f32)
    inp['w_in'] = nrm(ks[8], (DEPTH, d, N_IN), f32) * d ** -0.5
    inp['gla_w2'] = nrm(ks[9], (DEPTH, GLA_GATE_RANK, GLA_QK), f32) * GLA_GATE_RANK ** -0.5
    inp['gla_b2'] = 0.1 * nrm(ks[10], (DEPTH, GLA_QK), f32)
    inp['gla_norm_g'] = 1.0 + 0.02 * nrm(ks[11], (DEPTH, GLA_V), f32)
    inp['conv_w'] = nrm(ks[12], (DEPTH, CONV_W, 2 * ML_W), f32) * CONV_W ** -0.5
    inp['conv_b'] = 0.02 * nrm(ks[13], (DEPTH, 2 * ML_W), f32)
    inp['ml_i_b'] = 0.1 * nrm(ks[14], (DEPTH, ML_HEADS), f32)
    inp['ml_f_b'] = (jnp.linspace(3.0, 6.0, ML_HEADS, dtype=f32)[None, :]
                     + 0.1 * nrm(ks[15], (DEPTH, ML_HEADS), f32))
    inp['ml_norm_g'] = 1.0 + 0.02 * nrm(ks[16], (DEPTH, ML_W), f32)
    inp['w_out'] = nrm(ks[17], (DEPTH, d, d), f32) * d ** -0.5
    inp['norm2_g'] = 1.0 + 0.02 * nrm(ks[18], (DEPTH, d), f32)
    inp['peer_wq'] = nrm(ks[19], (DEPTH, d, PEER_HEADS * PEER_DQ), f32) * d ** -0.5
    inp['peer_subkeys'] = nrm(ks[20], (DEPTH, 2, N_KEYS, PEER_DQ // 2), f32) * (PEER_DQ // 2) ** -0.5
    inp['peer_u'] = nrm(ks[21], (DEPTH, N_EXPERTS, d), f32) * d ** -0.5
    inp['peer_v'] = nrm(ks[22], (DEPTH, N_EXPERTS, d), f32) * PEER_HEADS ** -0.5
    inp['final_g'] = 1.0 + 0.02 * nrm(ks[23], (d,), f32)
    return inp

def reference(x_prompt, x_sample, state_gla, state_mlstm_c, state_mlstm_n, state_mlstm_m,
              state_conv, norm1_g, w_in, gla_w2, gla_b2, gla_norm_g, conv_w, conv_b,
              ml_i_b, ml_f_b, ml_norm_g, w_out, norm2_g, peer_wq, peer_subkeys,
              peer_u, peer_v, final_g):
    bp = x_prompt.shape[0]
    dt = x_prompt.dtype
    z_gla = jnp.zeros((DEPTH, bp, GLA_HEADS, GLA_DK, GLA_DV), dt)
    z_c = jnp.zeros((DEPTH, bp, ML_HEADS, ML_DH, ML_DH), dt)
    z_n = jnp.zeros((DEPTH, bp, ML_HEADS, ML_DH), dt)
    z_m = jnp.zeros((DEPTH, bp, ML_HEADS), dt)
    z_conv = jnp.zeros((DEPTH, bp, CONV_W - 1, 2 * ML_W), dt)
    y_prompt, p_gla, p_c, p_n, p_m, p_conv = _trunk(
        x_prompt, z_gla, z_c, z_n, z_m, z_conv,
        norm1_g, w_in, gla_w2, gla_b2, gla_norm_g, conv_w, conv_b, ml_i_b, ml_f_b,
        ml_norm_g, w_out, norm2_g, peer_wq, peer_subkeys, peer_u, peer_v, final_g)
    y_sample, s_gla, s_c, s_n, s_m, s_conv = _trunk(
        x_sample, state_gla, state_mlstm_c, state_mlstm_n, state_mlstm_m, state_conv,
        norm1_g, w_in, gla_w2, gla_b2, gla_norm_g, conv_w, conv_b, ml_i_b, ml_f_b,
        ml_norm_g, w_out, norm2_g, peer_wq, peer_subkeys, peer_u, peer_v, final_g)
    return (y_prompt, y_sample, p_gla, p_c, p_n, p_m, p_conv, s_gla, s_c, s_n, s_m, s_conv)


_drawn_inputs = setup_inputs


def setup_inputs(seed=0):
    import zlib

    import numpy as np

    out = dict(_drawn_inputs(seed))
    spreads = {}
    factors = {'gla_norm_g': 43.977, 'ml_norm_g': 48.198, 'final_g': 24.081, 'norm2_g': 13.971}
    for name, (base, spread) in spreads.items():
        noise = np.random.default_rng([zlib.crc32(name.encode()), seed]).standard_normal(out[name].shape)
        drawn = base * np.exp(spread * noise) if base else spread * noise
        out[name] = jnp.asarray(drawn.astype(out[name].dtype))
    for name, factor in factors.items():
        out[name] = (out[name] * factor).astype(out[name].dtype)
    return out
```

```python
from contextlib import ExitStack

import concourse.bass as bass
from concourse import mybir

F32 = mybir.dt.float32
U32 = mybir.dt.uint32
I32 = mybir.dt.int32
ALU = mybir.AluOpType
ACT = mybir.ActivationFunctionType
AX_X = mybir.AxisListType.X

P = 128
D = 1024
T = 1024
NS = 8
HEADS = 4
DK = 128
DV = 256
KT = D // P
CHUNKS = T // P
TAU = 16.0
EPS = 1e-6
CONV = 4
MLW = 1024
C_AQ, C_AK, C_AV, C_AG, C_LR = 0, 512, 1024, 2048, 3072
C_BQ, C_BK, C_BV, C_BI, C_BF = 3088, 4112, 5136, 6160, 6164
C_BO, C_GA, C_GB = 6168, 7192, 8216
RANK = 16
PH = 8
NK = 128
TOPK = 16
SLOTS = PH * TOPK
NEG = -3.0e38


def done(count):
    return count + 2


class Chain:

    def __init__(self, eng, sem, per_step=0, mark=None):
        self.eng, self.sem, self.per_step, self.mark = eng, sem, per_step, mark
        self.base, self.count = 0, 0

    def step(self, n):
        self.base, self.count = n * self.per_step, 0

    def __call__(self, ins):
        self.count += 1
        ins.then_inc(self.sem, 1)
        self.eng.wait_ge(self.sem, self.base + self.count)
        if self.mark is not None:
            self.eng.sem_inc(self.mark, 1)

    def end(self):
        assert self.count == self.per_step, (self.count, self.per_step)


def bc(ap, axis, n):
    a = ap.unsqueeze(axis)
    shape = list(a.shape)
    shape[axis] = n
    return a.to_broadcast(shape)


def rsqrt_mean(chain, eng, stat, n):
    v, y, u = stat[:, 1:2], stat[:, 2:3], stat[:, 3:4]
    chain(eng.tensor_scalar(v, stat[:, 0:1], 1.0 / n, EPS, ALU.mult, ALU.add))
    chain(eng.tensor_scalar(y.bitcast(I32), v.bitcast(I32), -0.5, float(0x5F3759DF), ALU.mult, ALU.add))
    for turn in range(3):
        chain(eng.tensor_scalar(u, y, v, y, ALU.mult, ALU.mult))
        chain(eng.tensor_scalar(u, u, -0.5, 1.5, ALU.mult, ALU.add))
        last = eng.tensor_scalar(y, y, u, None, ALU.mult)
        if turn < 2:
            chain(last)
    return last


def rsqrt_pair(chain, eng, stat, n):
    v, y, u = stat[:, 1, :], stat[:, 2, :], stat[:, 3, :]
    chain(eng.tensor_scalar(v, stat[:, 0, :], 1.0 / n, EPS, ALU.mult, ALU.add))
    chain(eng.tensor_scalar(y.bitcast(I32), v.bitcast(I32), -0.5, float(0x5F3759DF), ALU.mult, ALU.add))
    for turn in range(3):
        chain(eng.tensor_tensor(u, y, y, ALU.mult))
        chain(eng.tensor_tensor(u, u, v, ALU.mult))
        chain(eng.tensor_scalar(u, u, -0.5, 1.5, ALU.mult, ALU.add))
        last = eng.tensor_tensor(y, y, u, ALU.mult)
        if turn < 2:
            chain(last)
    return last
def norm1_and_gates(nc, io, res):
    used = []
    with ExitStack() as ctx:
        def sb(name, shape, dt=F32):
            return ctx.enter_context(nc.sbuf_tensor("a_" + name, shape, dt))

        def psum(name, shape):
            return ctx.enter_context(nc.psum_tensor("a_" + name, shape, F32))

        def sem(name):
            used.append(nc.alloc_semaphore(name=name))
            return used[-1]

        x = sb("x", [P, 2, D])
        squares = sb("squares", [P, D])
        xn = sb("xn", [P, D])
        stat = sb("stat", [P, 2, 4])
        g1 = sb("g1", [P, KT])
        w_lr = sb("w_lr", [P, KT, RANK])
        w_if = sb("w_if", [P, KT, 2 * HEADS])
        w2 = sb("w2", [RANK, HEADS * DK])
        b2 = sb("b2", [P, HEADS])
        ib = sb("ib", [HEADS, 1])
        fb = sb("fb", [HEADS, 1])
        m0s = sb("m0s", [HEADS, NS])
        hc = sb("hc", [P, 2, KT, P])
        ones = sb("ones", [P, P])
        lrT = sb("lrT", [RANK, P])
        li = sb("li", [HEADS, P])
        zf = sb("zf", [HEADS, P])
        ef = sb("ef", [HEADS, P])
        lf = sb("lf", [HEADS, P])
        bsum = sb("bsum", [HEADS, P])
        cmax = sb("cmax", [HEADS, 2, P])
        mt = sb("mt", [HEADS, P])
        negm = sb("negm", [HEADS, 1])
        mrun = sb("mrun", [HEADS, 2])
        za = sb("za", [P, HEADS, P])
        ea = sb("ea", [P, HEADS, P])
        rows = sb("rows", [P, P])
        decay = sb("decay", [P, 2, HEADS, P])

        xT_ps = psum("xT_ps", [P, KT, P])
        if_ps = psum("if_ps", [RANK, 3, P])
        za_ps = psum("za_ps", [P, HEADS, P])
        rT_ps = psum("rT_ps", [P, P])

        params_loaded = sem("a_params_loaded")
        consts_done = sem("a_consts_done")
        ident_done = sem("a_ident_done")
        x_loaded = [sem(f"a_x_loaded{b}") for b in range(2)]
        squares_done = sem("a_squares_done")
        rstd_done = sem("a_rstd_done")
        xn_done = sem("a_xn_done")
        xT_done = sem("a_xT_done")
        hc_done = sem("a_hc_done")
        hc_stored = [sem(f"a_hc_stored{b}") for b in range(2)]
        if_done = sem("a_if_done")
        lr_done = sem("a_lr_done")
        za_mm_done = sem("a_za_mm_done")
        z_done = sem("a_z_done")
        ln_done = sem("a_ln_done")
        m_done = sem("a_m_done")
        rows_done = sem("a_rows_done")
        rT_done = sem("a_rT_done")
        cols_done = sem("a_cols_done")
        m_stored = [sem(f"a_m_stored{b}") for b in range(2)]
        dve_norm_order = sem("a_dve_norm_order")
        dve_order = sem("a_dve_order")
        act_order = sem("a_act_order")
        last_stored = sem("a_last_stored")

        x_p = io["x_prompt"]
        x_s = io["x_sample"]
        w_in = io["w_in"].rearrange("(k p) n -> p k n", p=P)
        block = ctx.enter_context(nc.Block())

        def chunks(eng, norm, gates):
            norm(0, 0, P, 0)
            with eng.Fori(0, CHUNKS // 2 - 1) as j:
                norm(2 * j + 1, 1, P, j)
                gates(2 * j, 0, P, j)
                norm(2 * j + 2, 0, P, j + 1)
                gates(2 * j + 1, 1, P, j)
            norm(CHUNKS - 1, 1, P, CHUNKS // 2 - 1)
            gates(CHUNKS - 2, 0, P, CHUNKS // 2 - 1)
            norm(CHUNKS, 0, NS, CHUNKS // 2)
            gates(CHUNKS - 1, 1, P, CHUNKS // 2 - 1)
            gates(CHUNKS, 0, NS, CHUNKS // 2)

        @block.gpsimd
        def _(pool):
            ident, mask = res["ident"], res["upper"]
            nc.gpsimd.memset(ident[:], 0.0).then_inc(ident_done, 1)
            nc.gpsimd.memset(rows[:], 0.0).then_inc(consts_done, 1)
            nc.gpsimd.memset(ones[:], 1.0).then_inc(consts_done, 1)
            nc.gpsimd.memset(mrun[:], 0.0).then_inc(consts_done, 1)
            nc.gpsimd.memset(res["eye8"][:], 0.0).then_inc(ident_done, 1)
            pool.wait_ge(ident_done, 2)
            pool.wait_ge(consts_done, 2)
            nc.gpsimd.affine_select(out=ident[:], in_=ident[:], compare_op=ALU.not_equal, fill=1.0,
                                    base=0, pattern=[[-1, P]], channel_multiplier=1).then_inc(ident_done, 1)
            nc.gpsimd.affine_select(out=mask[:], in_=ones[:], compare_op=ALU.is_ge, fill=0.0,
                                    base=0, pattern=[[1, P]], channel_multiplier=-1).then_inc(ident_done, 1)
            nc.gpsimd.affine_select(out=res["eye8"][:], in_=res["eye8"][:], compare_op=ALU.not_equal, fill=1.0,
                                    base=0, pattern=[[-1, NS], [1, NS]], channel_multiplier=0).then_inc(ident_done, 1)

        @block.sync
        def _(sp):
            sp.dma_start(x[:, 0, :], x_p[0:P, :]).then_inc(x_loaded[0], 16)
            sp.dma_start(x[:, 1, :], x_p[P:2 * P, :]).then_inc(x_loaded[1], 16)
            sp.dma_start(g1[:], io["norm1_g"].rearrange("(k p) -> p k", p=P)).then_inc(params_loaded, 16)
            sp.dma_start(w_lr[:], w_in[:, :, C_LR:C_LR + RANK]).then_inc(params_loaded, 16)
            sp.dma_start(w_if[:], w_in[:, :, C_BI:C_BI + 2 * HEADS]).then_inc(params_loaded, 16)
            sp.dma_start(w2[:], io["gla_w2"]).then_inc(params_loaded, 16)
            sp.dma_start(b2[:], io["gla_b2"].rearrange("(h p) -> p h", p=P)).then_inc(params_loaded, 16)
            sp.dma_start(ib[:], io["ml_i_b"].rearrange("(h a) -> h a", a=1)).then_inc(params_loaded, 16)
            sp.dma_start(fb[:], io["ml_f_b"].rearrange("(h a) -> h a", a=1)).then_inc(params_loaded, 16)
            sp.dma_start(m0s[:], io["state_mlstm_m"].rearrange("b h -> h b")).then_inc(params_loaded, 16)

            def store(n, b):
                sp.wait_ge(hc_done, done(n + 1))
                sp.dma_start(res["hT_d"][bass.ds(n, 1)].rearrange("a p f -> (a p) f"),
                             hc[:, b].rearrange("p k t -> p (k t)")).then_inc(hc_stored[b], 16)
                sp.wait_ge(rows_done, done(n + 1))
                sp.dma_start(res["m_d"][:, bass.ds(n * P, P)], cmax[:, b, :]).then_inc(m_stored[b], 16)
                sp.dma_start(res["decay_d"][bass.ds(n, 1)].rearrange("a p f -> (a p) f"),
                             decay[:, b].rearrange("p h t -> p (h t)")).then_inc(m_stored[b], 16)
                sp.dma_start(res["fc_d"][:, bass.ds(n, 1)], rows[32:32 + HEADS, P - 1:P]).then_inc(m_stored[b], 16)

            with sp.Fori(0, CHUNKS // 2 - 1) as j:
                for b in range(2):
                    sp.wait_ge(xn_done, done(2 * j + b + 1))
                    sp.dma_start(x[:, b, :], x_p[bass.ds((2 * j + b + 2) * P, P), :]).then_inc(x_loaded[b], 16)
                    store(2 * j + b, b)
            sp.wait_ge(xn_done, done(CHUNKS - 1))
            sp.dma_start(x[0:NS, 0, :], x_s).then_inc(x_loaded[0], 16)
            store(CHUNKS - 2, 0)
            store(CHUNKS - 1, 1)
            sp.wait_ge(cols_done, done(CHUNKS + 1))
            sp.dma_start(io["p_m"].rearrange("(h a) -> h a", a=1), mrun[:, 0:1]).then_inc(last_stored, 16)
            sp.dma_start(io["s_m"].rearrange("b h -> h b"), mt[:, 0:NS]).then_inc(last_stored, 16)
            sp.dma_start(res["fs_d"][:, :], rows[32:32 + HEADS, 0:NS]).then_inc(last_stored, 16)
            sp.wait_ge(last_stored, 48)
            for b in range(2):
                sp.wait_ge(hc_stored[b], 16 * (CHUNKS // 2) + 16)
                sp.wait_ge(m_stored[b], 48 * (CHUNKS // 2) + 48)

        @block.scalar
        def _(act):
            chain = Chain(act, act_order, 2)
            for s in (squares_done, xn_done, ln_done, rows_done):
                act.sem_inc(s, 2)
            act.preload_act_table_set("natural_log_exp_and_others")
            act.wait_ge(consts_done, 3)

            def norm(n, b, r, turn):
                act.wait_ge(x_loaded[b], 16 * (turn + 1))
                nc.scalar.activation(squares[0:r, :], x[0:r, b, :], ACT.Square,
                                     accum_out=stat[0:r, b, 0:1]).then_inc(squares_done, 1)
                act.wait_ge(rstd_done, done(n + 1))
                act.wait_ge(xT_done, done(n))
                nc.scalar.activation(xn[0:r, :], x[0:r, b, :], ACT.Copy,
                                     scale=stat[0:r, b, 2:3]).then_inc(xn_done, 1)

            def gates(n, b, w, turn):
                chain.step(n)
                sample = w == NS
                if sample:
                    act.wait_ge(m_stored[1], 48 * (CHUNKS // 2) + 48)
                act.wait_ge(z_done, done(n + 1))
                chain(nc.scalar.activation(ef[:, 0:w], ef[:, 0:w], ACT.Exp))
                nc.scalar.activation(ef[:, 0:w], ef[:, 0:w], ACT.Ln, bias=1.0)
                chain(nc.scalar.activation(ea[:, :, 0:w], ea[:, :, 0:w], ACT.Exp))
                nc.scalar.activation(ea[:, :, 0:w], ea[:, :, 0:w], ACT.Ln, bias=1.0).then_inc(ln_done, 1)
                act.wait_ge(m_done, done(n + 1))
                if sample:
                    nc.scalar.activation(rows[32:32 + HEADS, 0:w], bsum[:, 0:w], ACT.Exp)
                    nc.scalar.activation(rows[64:64 + HEADS, 0:w], mt[:, 0:w], ACT.Exp, scale=-1.0)
                    nc.scalar.activation(rows[96:96 + HEADS, 0:w], cmax[:, 0, 0:w], ACT.Exp).then_inc(rows_done, 1)
                else:
                    act.wait_ge(m_stored[1 - b], 48 * (turn + b) + 48)
                    nc.scalar.activation(rows[32:32 + HEADS, 0:w], cmax[:, b, :], ACT.Exp, scale=-1.0,
                                         bias=mrun[:, b:b + 1])
                    nc.scalar.activation(rows[64:64 + HEADS, 0:w], mt[:, 0:w], ACT.Exp, scale=-1.0)
                    nc.scalar.activation(rows[96:96 + HEADS, 0:w], rows[0:HEADS, :], ACT.Exp,
                                         bias=negm[:, 0:1]).then_inc(rows_done, 1)

            chunks(act, norm, gates)

        @block.tensor
        def _(pe):
            ident = res["ident"]
            for s in (xT_done, if_done, za_mm_done, rT_done):
                pe.sem_inc(s, 2)
            pe.wait_ge(ident_done, 5)
            pe.wait_ge(params_loaded, 128)

            def norm(n, b, r, turn):
                pe.wait_ge(xn_done, done(n + 1))
                pe.wait_ge(hc_done, done(n))
                for k in range(KT):
                    last = nc.tensor.transpose(xT_ps[:, k, 0:r], xn[0:r, k * P:(k + 1) * P], ident[0:r, 0:r])
                last.then_inc(xT_done, 1)

            def gates(n, hb, w, turn):
                sample = w == NS
                pe.wait_ge(hc_done, done(n + 1))
                h = res["hTs"] if sample else hc[:, hb]
                for q, (wt, lo, m) in enumerate(((w_lr, 0, RANK), (w_if, 0, HEADS), (w_if, HEADS, HEADS))):
                    for k in range(KT):
                        last = nc.tensor.matmul(if_ps[0:m, q, 0:w], wt[:, k, lo:lo + m], h[:, k, 0:w],
                                                start=(k == 0), stop=(k == KT - 1))
                last.then_inc(if_done, 1)
                pe.wait_ge(lr_done, done(n + 1))
                for h4 in range(HEADS):
                    last = nc.tensor.matmul(za_ps[:, h4, 0:w], w2[:, h4 * DK:(h4 + 1) * DK], lrT[:, 0:w],
                                            start=True, stop=True)
                last.then_inc(za_mm_done, 1)
                pe.wait_ge(rows_done, done(n + 1))
                nc.tensor.transpose(rT_ps[0:w, :], rows[:, 0:w], ident[:]).then_inc(rT_done, 1)

            chunks(pe, norm, gates)

        @block.vector
        def _(dve):
            for s in (rstd_done, hc_done, lr_done, z_done, m_done, cols_done):
                dve.sem_inc(s, 2)
            for b in range(2):
                dve.sem_inc(hc_stored[b], 16)
                dve.sem_inc(m_stored[b], 48)
            norm_chain = Chain(dve, dve_norm_order, 10)
            chain = Chain(dve, dve_order, 10)
            dve.wait_ge(params_loaded, 128)
            dve.wait_ge(consts_done, 3)

            def norm(n, b, w, turn):
                norm_chain.step(n)
                sample = w == NS
                dve.wait_ge(squares_done, done(n + 1))
                rsqrt_mean(norm_chain, nc.vector, stat[0:w, b], D).then_inc(rstd_done, 1)
                norm_chain.end()
                dve.wait_ge(xT_done, done(n + 1))
                h = res["hTs"] if sample else hc[:, b]
                if not sample:
                    dve.wait_ge(hc_stored[b], 16 * turn + 16)
                nc.vector.tensor_tensor(h[:, :, 0:w], xT_ps[:, :, 0:w], bc(g1[:], 2, w), ALU.mult).then_inc(hc_done, 1)

            def gates(n, b, w, turn):
                chain.step(n)
                sample = w == NS
                dve.wait_ge(if_done, done(n + 1))
                nc.vector.tensor_copy(lrT[:, 0:w], if_ps[0:RANK, 0, 0:w]).then_inc(lr_done, 1)
                nc.vector.tensor_scalar(li[:, 0:w], if_ps[0:HEADS, 1, 0:w], ib[:, 0:1], None, ALU.add)
                chain(nc.vector.tensor_scalar(zf[:, 0:w], if_ps[0:HEADS, 2, 0:w], fb[:, 0:1], None, ALU.add))
                chain(nc.vector.scalar_tensor_tensor(out=ef[:, 0:w], in0=zf[:, 0:w], scalar=-1.0, in1=zf[:, 0:w],
                                                     op0=ALU.mult, op1=ALU.min))
                dve.wait_ge(za_mm_done, done(n + 1))
                chain(nc.vector.tensor_tensor(za[:, :, 0:w], za_ps[:, :, 0:w], bc(b2[:], 2, w), ALU.add))
                nc.vector.scalar_tensor_tensor(out=ea[:, :, 0:w], in0=za[:, :, 0:w], scalar=-1.0, in1=za[:, :, 0:w],
                                               op0=ALU.mult, op1=ALU.min).then_inc(z_done, 1)
                dve.wait_ge(ln_done, done(n + 1))
                chain(nc.vector.scalar_tensor_tensor(out=lf[:, 0:w], in0=zf[:, 0:w], scalar=0.0, in1=ef[:, 0:w],
                                                     op0=ALU.min, op1=ALU.subtract))
                chain(nc.vector.scalar_tensor_tensor(out=za[:, :, 0:w], in0=za[:, :, 0:w], scalar=0.0,
                                                     in1=ea[:, :, 0:w], op0=ALU.min, op1=ALU.subtract))
                if sample:
                    dve.wait_ge(m_stored[0], 48 * turn + 48)
                    chain(nc.vector.tensor_tensor(lf[:, 0:w], lf[:, 0:w], m0s[:], ALU.add))
                    chain(nc.vector.tensor_tensor(mt[:, 0:w], lf[:, 0:w], li[:, 0:w], ALU.max))
                    nc.vector.tensor_tensor(bsum[:, 0:w], lf[:, 0:w], mt[:, 0:w], ALU.subtract)
                    chain(nc.vector.tensor_tensor(cmax[:, 0, 0:w], li[:, 0:w], mt[:, 0:w], ALU.subtract))
                    nc.vector.tensor_copy(res["lsig_s"][:], za[:, :, 0:w]).then_inc(m_done, 1)
                    dve.wait_ge(rT_done, done(n + 1))
                    nc.vector.tensor_copy(res["gates_s"][:].rearrange("t (q h) -> t q h", q=4),
                                          rT_ps[0:w, :].rearrange("t (q h) -> t q h", q=4)[:, :, 0:HEADS])\
                        .then_inc(cols_done, 1)
                    return
                chain(nc.vector.tensor_tensor_scan(bsum[:], ones[0:HEADS, :], lf[:], 0.0, ALU.mult, ALU.add))
                dve.wait_ge(rT_done, done(n))
                dve.wait_ge(m_stored[b], 48 * turn + 48)
                chain(nc.vector.tensor_tensor(rows[0:HEADS, :], li[:], bsum[:], ALU.subtract))
                chain(nc.vector.tensor_tensor_scan(cmax[:, b, :], rows[0:HEADS, :], rows[0:HEADS, :],
                                                   mrun[:, b:b + 1], ALU.max, ALU.max))
                chain(nc.vector.tensor_tensor(mt[:], bsum[:], cmax[:, b, :], ALU.add))
                nc.vector.tensor_scalar(negm[:], cmax[:, b, P - 1:P], -1.0, None, ALU.mult)
                chain(nc.vector.tensor_copy(mrun[:, 1 - b:2 - b], mt[:, P - 1:P]))
                for h4 in range(HEADS):
                    last = nc.vector.tensor_tensor_scan(
                        decay[:, b, h4, :], ones[:], za[:, h4, :], 0.0, ALU.mult, ALU.add)
                last.then_inc(m_done, 1)
                dve.wait_ge(rT_done, done(n + 1))
                nc.vector.tensor_copy(res["gates"][:, bass.ds(n, 1), :].rearrange("t a (q h) -> t (a q) h", q=4),
                                      rT_ps[:].rearrange("t (q h) -> t q h", q=4)[:, :, 0:HEADS]).then_inc(cols_done, 1)
                chain.end()

            chunks(dve, norm, gates)
    nc.clear_and_free_semaphores(used)
    nc.all_engine_barrier()


GROUPS = (((C_AQ, DK), (C_AK, DK), (C_AV, DV)), ((C_BQ, DV), (C_BK, DV)), ((C_AG, DV), (C_GA, DV)),
          ((C_BO, DV), (C_GB, DV)), ((C_BV, DV),))
NG = len(GROUPS)
WIDTH = [sum(w for _, w in g) for g in GROUPS]
SUB = 32
NSUB = P // SUB
CLAMP = 40.0
GLA_SCALE = float(DK) ** -0.5
ML_SCALE = float(DV) ** -0.5


def mixer(nc, io, res):
    with ExitStack() as ctx:
        def sb(name, shape, dt=F32):
            return ctx.enter_context(nc.sbuf_tensor("b_" + name, shape, dt))

        def psum(name, shape):
            return ctx.enter_context(nc.psum_tensor("b_" + name, shape, F32))

        def sem(name):
            return ctx.enter_context(nc.semaphore(name))

        w = [sb(f"w{g}", [P, KT, WIDTH[g]]) for g in range(NG)]
        hc = sb("hcB", [P, 2, KT, P])
        qkv = sb("qkv", [P, 2, 2 * DK + DV])
        bqk = sb("bqk", [P, 2, 2 * DV])
        v1 = sb("v1", [P, DV + 1])
        eA = sb("eA", [P, 2 * DV])
        eB = sb("eB", [P, 2 * DV])
        gateA = sb("gateA", [P, 2, DV])
        gateB = sb("gateB", [P, 2, DV])
        gtmp = sb("gtmp", [P, DV])
        gainA = sb("gainA", [P, DV])
        gainB = sb("gainB", [P, DV])
        dcy = sb("dcy", [P, 2, P])
        refs = sb("refs", [P, NSUB + 1])
        dif = sb("dif", [P, NSUB + 2, P])
        e0 = sb("e0", [P, P])
        kI = sb("kI", [P, NSUB + 1, P])
        qI = sb("qI", [P, P])
        q0 = sb("q0", [P, P])
        attT = sb("attT", [P, P])
        klast = sb("klast", [P, P])
        S = sb("S", [P, DV])
        taps_all = sb("taps_all", [P, 2, 2 * HEADS, CONV + 1])
        taps = sb("taps", [P, 2, 2, CONV + 1])
        cbuf = sb("cbuf", [P, 2, 4, CONV - 1 + P])
        y = sb("y", [P, 4, P])
        ey = sb("ey", [P, 4, P])
        qkT = sb("qkT", [P, 4, P])
        mb = sb("mb", [P, 2, P])
        fcb = sb("fcb", [P, 2, 1])
        gc = sb("gc", [P, 2, 4])
        pw = sb("pw", [P, P])
        sT = sb("sT", [P, P])
        kw = sb("kw", [P, DV])
        inter = sb("inter", [P, DV + 1])
        num = sb("num", [P, DV + 1])
        C = sb("C", [P, 2, DV + 1])
        den = sb("den", [P, 4])
        sq = sb("sq", [P, 2, DV])
        stat = sb("statB", [P, 4, 2])
        comb = sb("comb", [P, 1])
        mixA = sb("mixA", [P, DV])
        mix = sb("mix", [P, DV])
        mT = sb("mT", [P, 2, 2, P])
        s_qkv = sb("s_qkv", [NS, 2 * DK + DV])
        s_bqk = sb("s_bqk", [NS, 2 * DV])
        s_v = sb("s_v", [NS, DV])
        s_gateA = sb("s_gateA", [NS, DV])
        s_gateB = sb("s_gateB", [NS, DV])
        s_hist = sb("s_hist", [NS, CONV - 1, 2 * DV])
        s_taps = sb("s_taps", [NS, CONV + 1, 2 * DV])
        s_qk = sb("s_qk", [NS, 2 * DV])
        s_kw = sb("s_kw", [NS, DV])
        s_qd = sb("s_qd", [P, 3, NS, NS])
        s_S = sb("s_S", [P, NS, DV])
        s_C = sb("s_C", [P, NS, 2, DV])
        s_n = sb("s_n", [NS, DV])
        s_f = sb("s_f", [P, NS])
        s_a_all = sb("s_a_all", [P, HEADS, NS])
        s_a = sb("s_a", [P, NS])
        s_gc = sb("s_gc", [NS, 4])
        s_den = sb("s_den", [NS, 4])
        s_stat = sb("s_stat", [NS, 4, 2])
        s_comb = sb("s_comb", [NS, 1])
        s_work = sb("s_work", [NS, NS, DV])
        s_prod = s_work[:].rearrange("t a b -> t (a b)")[:, 0:(CONV - 1) * 2 * DV]\
            .rearrange("t (a b) -> t a b", a=CONV - 1)
        s_kwm = s_work
        s_km = s_taps[:].rearrange("t a b -> t (a b)")[:, 0:NS * DK].rearrange("t (a b) -> t a b", a=NS)
        s_eA, s_eB = eA[0:NS, :], eB[0:NS, :]
        s_y, s_ey = (v[0:NS].rearrange("t a b -> t (a b)") for v in (y, ey))
        s_qn, s_mixA, s_mix, s_num = mixA[0:NS, :], mixA[0:NS, :], mix[0:NS, :], num[0:NS, 0:DV]

        pj = [psum(f"pj{i}", [P, 512]) for i in range(2)]
        trB = psum("trB", [P, 512])
        trA = psum("trA", [P, 512])
        p4 = psum("p4", [P, 512])
        pnum = psum("pnum", [P, 512])
        pint = psum("pint", [P, 512])
        pgla = psum("pgla", [P, 512])

        s_banks = [trB, trA, pnum, pint]

        w_loaded = [sem(f"b_w_loaded{g}") for g in range(NG)]
        h_loaded = [sem(f"b_h_loaded{b}") for b in range(2)]
        m_loaded = [sem(f"b_m_loaded{b}") for b in range(2)]
        params_loaded = sem("b_params_loaded")
        zeros_done = sem("b_zeros_done")
        head_ready = sem("b_head_ready")
        state_stored = sem("b_state_stored")
        conv_stored = sem("b_conv_stored")
        mix_stored = [sem(f"b_mix_stored{b}") for b in range(2)]
        proj_done = [sem(f"b_proj_done{g}") for g in range(NG)]
        evac_done = [sem(f"b_evac_done{g}") for g in range(NG)]
        exp_done = [sem(f"b_exp_done{g}") for g in range(NG)]
        t1_done = sem("b_t1_done")
        s2_done = sem("b_s2_done")
        s3_done = sem("b_s3_done")
        s4_done = sem("b_s4_done")
        slices_done = sem("b_slices_done")
        dif_done = sem("b_dif_done")
        dif_exp_done = sem("b_dif_exp_done")
        e0_done = sem("b_e0_done")
        pw_in_done = sem("b_pw_in_done")
        pw_exp_done = sem("b_pw_exp_done")
        cbuf_done = sem("b_cbuf_done")
        tap_done = sem("b_tap_done")
        y_done = sem("b_y_done")
        ey_done = sem("b_ey_done")
        s2_ready = sem("b_s2_ready")
        att_done = sem("b_att_done")
        s2_evac_done = sem("b_s2_evac_done")
        num_done = sem("b_num_done")
        squares_done = sem("b_squares_done")
        state_done = sem("b_state_done")
        mix_done = sem("b_mix_done")
        mT_done = sem("b_mT_done")
        dve_order = sem("b_dve_order")
        s_loaded = sem("b_s_loaded")
        s_state_loaded = sem("b_s_state_loaded")
        s_stored = sem("b_s_stored")
        s_proj_done = [sem(f"b_s_proj_done{g}") for g in range(NG)]
        s_evac_done = [sem(f"b_s_evac_done{g}") for g in range(NG)]
        s_exp_done = sem("b_s_exp_done")
        s_a_done = sem("b_s_a_done")
        s_y_done = sem("b_s_y_done")
        s_ey_done = sem("b_s_ey_done")
        s_qk_done = sem("b_s_qk_done")
        s_qT_done = sem("b_s_qT_done")
        s_masks_done = sem("b_s_masks_done")
        s_outer_done = [sem(f"b_s_outer_done{i}") for i in range(3)]
        s_update_done = [sem(f"b_s_update_done{i}") for i in range(3)]
        s_out_done = sem("b_s_out_done")
        s_num_done = sem("b_s_num_done")
        s_squares_done = sem("b_s_squares_done")
        s_mix_done = sem("b_s_mix_done")
        s_mT_done = sem("b_s_mT_done")
        s_end_done = sem("b_s_end_done")
        dve_sample_order = sem("b_dve_sample_order")
        dve_gateA_order = sem("b_dve_gateA_order")
        dve_gateB_order = sem("b_dve_gateB_order")
        gateB_done = sem("b_gateB_done")
        pe_mark = sem("b_pe_mark")
        sp_mark = sem("b_sp_mark")

        w_in = io["w_in"].rearrange("(k p) n -> p k n", p=P)
        block = ctx.enter_context(nc.Block())

        @block.gpsimd
        def _(pool):
            nc.gpsimd.memset(v1[:, DV:DV + 1], 1.0).then_inc(zeros_done, 1)
            nc.gpsimd.memset(attT[:], 0.0).then_inc(zeros_done, 1)
            with pool.Fori(0, HEADS) as h:
                for g in range(NG):
                    pool.wait_ge(proj_done[g], done(h * CHUNKS))
                    at = 0
                    for first, width in GROUPS[g]:
                        pool.dma_start(w[g][:, :, at:at + width], w_in[:, :, bass.ds(first + h * width, width)])\
                            .then_inc(w_loaded[g], 16)
                        at += width
            for g in range(NG):
                pool.wait_ge(w_loaded[g], 16 * len(GROUPS[g]) * HEADS)

        @block.sync
        def _(sp):
            def load_chunk(h, c, b):
                sp.dma_start(hc[:, b].rearrange("p k t -> p (k t)"),
                             res["hT_d"][bass.ds(c, 1)].rearrange("a p f -> (a p) f")).then_inc(h_loaded[b], 16)

            def load_gates(h, c, b):
                sp.dma_start(mb[:, b, :], res["m_d"][bass.ds(h, 1), bass.ds(c * P, P)].rearrange("a t -> (a t)")
                             .partition_broadcast(P)).then_inc(m_loaded[b], 16)
                sp.dma_start(dcy[:, b, :], res["decay_d"][bass.ds(c, 1), :, bass.ds(h * P, P)]
                             .rearrange("a p t -> (a p) t")).then_inc(m_loaded[b], 16)
                sp.dma_start(fcb[:, b, :], res["fc_d"][bass.ds(h, 1), bass.ds(c, 1)].rearrange("a t -> (a t)")
                             .partition_broadcast(P)).then_inc(m_loaded[b], 16)

            def store_mix(n, h, c, b):
                sp.wait_ge(mT_done, done(n + 1))
                sp.dma_start(res["mixT_d"][bass.ds(c, 1), :, bass.ds(2 * h, 2), :].rearrange("a p k t -> (a p) k t"),
                             mT[:, b]).then_inc(mix_stored[b], 16)

            def step(h, c, b, ahead):
                n = h * CHUNKS + c
                if ahead:
                    sp.wait_ge(proj_done[NG - 1], done(n + 1))
                    load_chunk(h, c + 2, b)
                    sp.wait_ge(state_done, done(n + 1))
                    load_gates(h, c + 2, b)
                store_mix(n, h, c, b)

            for a in range(2):
                for k in range(2 * HEADS):
                    lo = (a * 2 * HEADS + k) * P
                    sp.dma_start(taps_all[:, a, k, 0:CONV], io["conv_w"][:, lo:lo + P].rearrange("j p -> p j"))\
                        .then_inc(params_loaded, 16)
                sp.dma_start(taps_all[:, a, :, CONV:CONV + 1].rearrange("p k a -> p (k a)"),
                             io["conv_b"][a * MLW:(a + 1) * MLW].rearrange("(k p) -> p k", p=P))\
                    .then_inc(params_loaded, 16)
            def load_sample(h):
                for a in range(2):
                    cols = bass.ds(a * MLW + h * DV, DV)
                    to = slice(a * DV, (a + 1) * DV)
                    sp.dma_start(s_hist[:, :, to], io["state_conv"][:, :, cols]).then_inc(s_loaded, 16)
                    sp.dma_start(s_taps[:, 0:CONV, to], io["conv_w"][:, cols].partition_broadcast(NS))\
                        .then_inc(s_loaded, 16)
                    sp.dma_start(s_taps[:, CONV, to], io["conv_b"][cols].partition_broadcast(NS)).then_inc(s_loaded, 16)
                sp.wait_ge(gateB_done, done(h * CHUNKS))
                sp.sem_inc(sp_mark, 1)
                for gain, name in ((gainA, "gla_norm_g"), (gainB, "ml_norm_g")):
                    sp.dma_start(gain[:], io[name][bass.ds(h * DV, DV)].partition_broadcast(P)).then_inc(s_loaded, 16)
                for src, dst in (
                        (io["state_mlstm_n"][:, bass.ds(h, 1)].rearrange("b a k -> (a b) k"), s_n[:]),
                        (res["fs_d"][bass.ds(h, 1)].rearrange("a b -> (a b)").partition_broadcast(P), s_f[:])):
                    sp.dma_start(dst, src).then_inc(s_loaded, 16)
                sp.dma_start(s_S[:], io["state_gla"][:, bass.ds(h, 1)].rearrange("b a k v -> k (a b) v"))\
                    .then_inc(s_state_loaded, 16)
                for t in range(2):
                    sp.dma_start(s_C[:, :, t, :], io["state_mlstm_c"][:, bass.ds(h, 1), t * P:(t + 1) * P, :]
                                 .rearrange("b a p v -> p (a b) v")).then_inc(s_state_loaded, 16)

            def store_sample(h):
                sp.wait_ge(s_out_done, done(h + 1))
                sp.sem_inc(sp_mark, 1)
                sp.dma_start(io["s_gla"][:, bass.ds(h, 1)].rearrange("b a k v -> k (a b) v"), s_S[:])\
                    .then_inc(s_stored, 16)
                for t in range(2):
                    sp.dma_start(io["s_c"][:, bass.ds(h, 1), t * P:(t + 1) * P, :].rearrange("b a p v -> p (a b) v"),
                                 s_C[:, :, t, :]).then_inc(s_stored, 16)
                sp.wait_ge(s_num_done, done(h + 1))
                sp.sem_inc(sp_mark, 1)
                sp.dma_start(io["s_n"][:, bass.ds(h, 1)].rearrange("b a k -> (a b) k"), s_n[:]).then_inc(s_stored, 16)
                for a in range(2):
                    cols = bass.ds(a * MLW + h * DV, DV)
                    to = slice(a * DV, (a + 1) * DV)
                    sp.dma_start(io["s_conv"][:, 0:CONV - 2, cols], s_hist[:, 1:, to]).then_inc(s_stored, 16)
                    sp.dma_start(io["s_conv"][:, CONV - 2, cols], s_bqk[:, to]).then_inc(s_stored, 16)

            with sp.Fori(0, HEADS) as h:
                sp.wait_ge(s_stored, 128 * h + 128)
                sp.sem_inc(sp_mark, 1)
                sp.wait_ge(s_end_done, done(h))
                sp.sem_inc(sp_mark, 1)
                load_sample(h)
                sp.wait_ge(proj_done[NG - 1], done(h * CHUNKS))
                load_chunk(h, 0, 0)
                load_chunk(h, 1, 1)
                sp.wait_ge(state_done, done(h * CHUNKS))
                load_gates(h, 0, 0)
                load_gates(h, 1, 1)
                store_sample(h)
                with sp.Fori(0, CHUNKS // 2 - 1) as j:
                    for b in range(2):
                        step(h, 2 * j + b, b, True)
                step(h, CHUNKS - 2, 0, False)
                step(h, CHUNKS - 1, 1, False)
                sp.wait_ge(state_done, done(h * CHUNKS + CHUNKS))
                sp.dma_start(io["p_gla"][bass.ds(h, 1)].rearrange("a k v -> (a k) v"), S[:]).then_inc(state_stored, 16)
                sp.dma_start(io["p_c"][bass.ds(h, 1)].rearrange("a (t p) v -> p (a t) v", p=P), C[:, :, 0:DV])\
                    .then_inc(state_stored, 16)
                sp.dma_start(io["p_n"][bass.ds(h, 1)].rearrange("a (t p) -> p (a t)", p=P),
                             C[:, :, DV:DV + 1].rearrange("p t a -> p (t a)")).then_inc(state_stored, 16)
                for a in range(2):
                    sp.dma_start(io["p_conv"][:, bass.ds(a * MLW + h * DV, DV)],
                                 bqk[P - CONV + 1:P, 1, a * DV:(a + 1) * DV]).then_inc(conv_stored, 16)
            sp.wait_ge(state_stored, 48 * HEADS + 48)
            sp.wait_ge(conv_stored, 32 * HEADS + 32)
            sp.wait_ge(s_stored, 128 * HEADS + 128)
            for b in range(2):
                sp.wait_ge(mix_stored[b], 16 * (HEADS * CHUNKS // 2) + 16)

        @block.tensor
        def _(pe):
            ident = res["ident"]
            for s in proj_done + s_proj_done + s_outer_done + [t1_done, s2_done, s3_done, s4_done, s_qT_done,
                                                               s_out_done, s_mT_done]:
                pe.sem_inc(s, 2)
            pe.wait_ge(zeros_done, 2)

            def project(g, n, h, b, turn, first=False):
                if g == 0:
                    pe.wait_ge(h_loaded[b], 16 * turn + 16)
                pe.wait_ge(w_loaded[g], 16 * len(GROUPS[g]) * (h + 1))
                if g >= 2:
                    pe.wait_ge(evac_done[g - 2], done(n + 1))
                elif first:
                    pe.wait_ge(s_evac_done[4 - g], done(h + 1))
                else:
                    pe.wait_ge(evac_done[4 - g], done(n))
                for k in range(KT):
                    last = nc.tensor.matmul(pj[g % 2][:, 0:WIDTH[g]], hc[:, b, k, :], w[g][:, k, :],
                                            start=(k == 0), stop=(k == KT - 1))
                last.then_inc(proj_done[g], 1)

            def step(h, c, b, turn, turn1, first_head=None, next_head=None):
                n = h * CHUNKS + c
                if first_head is not None:
                    pe.wait_ge(s_end_done, done(first_head + 1))
                pe.wait_ge(evac_done[1], done(n + 1))
                pe.wait_ge(state_done, done(n))
                for t in range(4):
                    nc.tensor.transpose(trB[:, t * P:(t + 1) * P], bqk[:, b, t * P:(t + 1) * P], ident[:])
                for t in range(2):
                    last = nc.tensor.transpose(trA[:, t * P:(t + 1) * P], qkv[:, b, t * DK:(t + 1) * DK], ident[:])
                last.then_inc(t1_done, 1)
                if turn1 is not None:
                    project(0, n + 1, h, 1 - b, turn1)
                    project(1, n + 1, h, 1 - b, turn1)
                if next_head is not None:
                    project_sample(0, next_head)
                    project_sample(1, next_head)
                pe.wait_ge(s2_ready, done(n + 1))
                pe.wait_ge(mT_done, done(n))
                for i in range(NSUB):
                    m = (i + 1) * SUB
                    nc.tensor.matmul(trA[0:m, 256 + i * SUB:256 + (i + 1) * SUB], kI[:, i, 0:m],
                                     qI[:, i * SUB:(i + 1) * SUB], start=True, stop=True)
                nc.tensor.transpose(p4[:, 2 * P:3 * P], kI[:, NSUB, :], ident[:])
                for t in range(2):
                    nc.tensor.matmul(trA[:, 384:512], qkT[:, 2 + t, :], qkT[:, t, :], start=(t == 0), stop=(t == 1))
                for t in range(2):
                    nc.tensor.transpose(p4[:, t * P:(t + 1) * P], qkT[:, 2 + t, :], ident[:])
                for t in range(2):
                    last = nc.tensor.matmul(pint[:, 0:DV + 1], qkT[:, t, :], C[:, t, :], start=(t == 0), stop=(t == 1))
                last.then_inc(s2_done, 1)
                if turn1 is not None:
                    project(2, n + 1, h, 1 - b, turn1)
                pe.wait_ge(att_done, done(n + 1))
                pe.wait_ge(s2_evac_done, done(n + 1))
                pe.wait_ge(evac_done[4], done(n + 1))
                nc.tensor.matmul(pnum[:, 0:DV + 1], sT[:], v1[:], start=True, stop=True)
                nc.tensor.matmul(pgla[:, 0:DV], q0[:], S[:], start=True, stop=False)
                nc.tensor.matmul(pgla[:, 0:DV], attT[:], qkv[:, b, 2 * DK:], start=False, stop=True)
                nc.tensor.matmul(trA[:, 0:DV], klast[:], qkv[:, b, 2 * DK:], start=True, stop=True)
                nc.tensor.matmul(pint[:, 0:DV + 1], kw[:, 0:P], v1[:], start=True, stop=True)
                nc.tensor.matmul(trB[:, 0:DV + 1], kw[:, P:2 * P], v1[:], start=True, stop=True).then_inc(s3_done, 1)
                if turn1 is not None:
                    project(3, n + 1, h, 1 - b, turn1)
                    project(4, n + 1, h, 1 - b, turn1)
                pe.wait_ge(mix_done, done(n + 1))
                for t in range(2):
                    last = nc.tensor.transpose(p4[:, t * P:(t + 1) * P], mix[:, t * P:(t + 1) * P], ident[:])
                last.then_inc(s4_done, 1)

            def project_sample(g, h):
                pe.wait_ge(w_loaded[g], 16 * len(GROUPS[g]) * (h + 1))
                if g >= 2:
                    pe.wait_ge(s_evac_done[g - 2], done(h + 1))
                else:
                    pe.wait_ge(evac_done[4 - g], done(h * CHUNKS))
                for k in range(KT):
                    last = nc.tensor.matmul(pj[g % 2][0:NS, 0:WIDTH[g]], res["hTs"][:, k, :], w[g][:, k, :],
                                            start=(k == 0), stop=(k == KT - 1))
                last.then_inc(s_proj_done[g], 1)

            def outer(i, h):
                if i:
                    pe.wait_ge(s_update_done[i - 1], done(h + 1))
                for q in range(NS):
                    out = s_banks[q // 2][:, (q % 2) * DV:(q % 2 + 1) * DV]
                    if i == 0:
                        last = nc.tensor.matmul(out, s_km[:, q, :], s_qkv[:, 2 * DK:], start=True, stop=True)
                    else:
                        tok, t = (i - 1) * 4 + q // 2, q % 2
                        last = nc.tensor.matmul(out, s_kwm[:, tok, t * P:(t + 1) * P], s_v[:], start=True, stop=True)
                last.then_inc(s_outer_done[i], 1)

            def head(h, next_head):
                turn = h * (CHUNKS // 2)
                n0 = h * CHUNKS
                for g in range(2, NG):
                    project_sample(g, h)
                pe.wait_ge(head_ready, done(h + 1))
                pe.wait_ge(s_qk_done, done(h + 1))
                pe.sem_inc(pe_mark, 1)
                nc.tensor.transpose(trA[:, 0:NS], s_qkv[:, 0:DK], ident[0:NS, 0:NS])
                for t in range(2):
                    last = nc.tensor.transpose(trA[:, (1 + t) * NS:(2 + t) * NS], s_qk[:, t * P:(t + 1) * P],
                                               ident[0:NS, 0:NS])
                last.then_inc(s_qT_done, 1)
                project(0, n0, h, 0, turn, first=True)
                pe.wait_ge(s_masks_done, done(h + 1))
                outer(0, h)
                project(1, n0, h, 0, turn, first=True)
                pe.wait_ge(s_evac_done[4], done(h + 1))
                outer(1, h)
                project(2, n0, h, 0, turn)
                outer(2, h)
                project(3, n0, h, 0, turn)
                pe.wait_ge(s_update_done[2], done(h + 1))
                for q in range(NS):
                    nc.tensor.matmul(pgla[0:NS, 0:DV], s_qd[:, 0, q, :], s_S[:, q, :], start=(q == 0), stop=(q == NS - 1))
                for q in range(NS):
                    for t in range(2):
                        last = nc.tensor.matmul(pnum[0:NS, 0:DV], s_qd[:, 1 + t, q, :], s_C[:, q, t, :],
                                                start=(q + t == 0), stop=(q == NS - 1 and t == 1))
                last.then_inc(s_out_done, 1)
                project(4, n0, h, 0, turn)
                pe.wait_ge(s_mix_done, done(h + 1))
                pe.sem_inc(pe_mark, 1)
                for t in range(2):
                    last = nc.tensor.transpose(trA[:, t * NS:(t + 1) * NS], s_mix[:, t * P:(t + 1) * P],
                                               ident[0:NS, 0:NS])
                last.then_inc(s_mT_done, 1)
                with pe.Fori(0, CHUNKS // 2 - 1) as j:
                    step(h, 2 * j, 0, turn + j, turn + j, first_head=h)
                    step(h, 2 * j + 1, 1, turn + j, turn + j + 1)
                step(h, CHUNKS - 2, 0, turn + 3, turn + 3)
                step(h, CHUNKS - 1, 1, turn + 3, None, next_head=next_head)

            project_sample(0, 0)
            project_sample(1, 0)
            with pe.Fori(0, HEADS - 1) as h:
                head(h, h + 1)
            head(HEADS - 1, None)

        @block.scalar
        def _(act):
            for s in s_evac_done[0:2] + s_evac_done[3:] + [s_exp_done, s_a_done, s_ey_done, s_squares_done]:
                act.sem_inc(s, 2)
            for s in [evac_done[0], evac_done[1], evac_done[3], evac_done[4], exp_done[2], 
dif_exp_done, e0_done, pw_exp_done, tap_done, ey_done, s2_evac_done, squares_done, mT_done]:
                act.sem_inc(s, 2)

            def evacuate(g, n, b, turn):
                act.wait_ge(proj_done[g], done(n + 1))
                if g == 0:
                    act.wait_ge(s3_done, done(n - 1))
                    nc.scalar.activation(qkv[:, b, :], pj[0][:], ACT.Copy).then_inc(evac_done[0], 1)
                elif g == 1:
                    act.wait_ge(t1_done, done(n - 1))
                    nc.scalar.activation(bqk[:, b, :], pj[1][:], ACT.Copy).then_inc(evac_done[1], 1)
                elif g == 2:
                    act.wait_ge(evac_done[2], done(n))
                    nc.scalar.activation(eA[:], pj[0][:], ACT.Exp, scale=-1.0).then_inc(exp_done[2], 1)
                elif g == 3:
                    act.wait_ge(gateB_done, done(n))
                    nc.scalar.activation(eB[:], pj[1][:], ACT.Exp, scale=-1.0).then_inc(evac_done[3], 1)
                else:
                    act.wait_ge(s3_done, done(n))
                    nc.scalar.activation(v1[:, 0:DV], pj[0][:, 0:DV], ACT.Copy).then_inc(evac_done[4], 1)

            def step(h, c, b, turn, ahead):
                n = h * CHUNKS + c
                act.wait_ge(m_loaded[b], 48 * turn + 48)
                act.wait_ge(state_done, done(n))
                nc.scalar.activation(e0[:], dcy[:, b, :], ACT.Exp, scale=1.0 / TAU).then_inc(e0_done, 1)
                act.wait_ge(dif_done, done(n + 1))
                nc.scalar.activation(dif[:], dif[:], ACT.Exp, scale=1.0 / TAU).then_inc(dif_exp_done, 1)
                act.wait_ge(pw_in_done, done(n + 1))
                nc.scalar.activation(pw[:], pw[:], ACT.Exp, scale=-1.0).then_inc(pw_exp_done, 1)
                act.wait_ge(cbuf_done, done(n + 1))
                for t in range(4):
                    last = nc.scalar.activation(y[:, t, :], cbuf[:, b, t, 0:P], ACT.Identity,
                                                scale=taps[:, t // 2, t % 2, 0:1],
                                                bias=taps[:, t // 2, t % 2, CONV:CONV + 1])
                last.then_inc(tap_done, 1)
                act.wait_ge(y_done, done(n + 1))
                nc.scalar.activation(ey[:], y[:], ACT.Exp, scale=-1.0).then_inc(ey_done, 1)
                if ahead:
                    evacuate(0, n + 1, 1 - b, turn)
                    evacuate(1, n + 1, 1 - b, turn)
                act.wait_ge(s2_done, done(n + 1))
                act.wait_ge(num_done, done(n))
                nc.scalar.activation(kw[:], p4[:, 0:2 * P], ACT.Copy, scale=gc[:, b, 3:4])
                nc.scalar.activation(klast[:], p4[:, 2 * P:3 * P], ACT.Copy)
                nc.scalar.activation(inter[:], pint[:, 0:DV + 1], ACT.Copy, scale=gc[:, b, 1:2])\
                    .then_inc(s2_evac_done, 1)
                if ahead:
                    evacuate(2, n + 1, 1 - b, turn)
                act.wait_ge(s3_done, done(n + 1))
                nc.scalar.activation(sq[:, 0, :], pgla[:, 0:DV], ACT.Square, accum_out=stat[:, 0, 0:1])
                act.wait_ge(num_done, done(n + 1))
                nc.scalar.activation(sq[:, 1, :], num[:, 0:DV], ACT.Square, scale=den[:, 2:3], accum_out=stat[:, 0, 1:2])\
                    .then_inc(squares_done, 1)
                if ahead:
                    evacuate(3, n + 1, 1 - b, turn)
                    evacuate(4, n + 1, 1 - b, turn)
                act.wait_ge(s4_done, done(n + 1))
                act.wait_ge(mix_stored[b], 16 * turn + 16)
                nc.scalar.activation(mT[:, b].rearrange("p k t -> p (k t)"), p4[:, 0:2 * P], ACT.Copy)\
                    .then_inc(mT_done, 1)

            nc.scalar.activation(s_a_all[:], res["lsig_s"][:], ACT.Exp, scale=1.0 / TAU).then_inc(s_a_done, 1)
            with act.Fori(0, HEADS) as h:
                turn = h * (CHUNKS // 2)
                act.wait_ge(s_proj_done[0], done(h + 1))
                nc.scalar.activation(s_qkv[:], pj[0][0:NS, :], ACT.Copy).then_inc(s_evac_done[0], 1)
                act.wait_ge(s_proj_done[1], done(h + 1))
                act.wait_ge(s_stored, 128 * h + 128)
                nc.scalar.activation(s_bqk[:], pj[1][0:NS, :], ACT.Copy).then_inc(s_evac_done[1], 1)
                act.wait_ge(s_y_done, done(h + 1))
                nc.scalar.activation(s_ey, s_y, ACT.Exp, scale=-1.0).then_inc(s_ey_done, 1)
                act.wait_ge(s_proj_done[2], done(h + 1))
                act.wait_ge(evac_done[2], done(h * CHUNKS))
                nc.scalar.activation(s_eA, pj[0][0:NS, :], ACT.Exp, scale=-1.0).then_inc(s_exp_done, 1)
                act.wait_ge(s_proj_done[3], done(h + 1))
                act.wait_ge(gateB_done, done(h * CHUNKS))
                nc.scalar.activation(s_eB, pj[1][0:NS, :], ACT.Exp, scale=-1.0).then_inc(s_evac_done[3], 1)
                act.wait_ge(s_proj_done[4], done(h + 1))
                nc.scalar.activation(s_v[:], pj[0][0:NS, 0:DV], ACT.Copy).then_inc(s_evac_done[4], 1)
                act.wait_ge(conv_stored, 32 * h + 32)
                act.wait_ge(s_evac_done[2], done(h + 1))
                act.wait_ge(s_masks_done, done(h + 1))
                for g in range(NG):
                    if g == NG - 1:
                        act.wait_ge(s_out_done, done(h + 1))
                        nc.scalar.activation(sq[0:NS, 0, :], pgla[0:NS, 0:DV], ACT.Square, accum_out=s_stat[:, 0, 0:1])
                        act.wait_ge(s_num_done, done(h + 1))
                        nc.scalar.activation(sq[0:NS, 1, :], s_num, ACT.Square, scale=s_den[:, 2:3],
                                             accum_out=s_stat[:, 0, 1:2]).then_inc(s_squares_done, 1)
                    evacuate(g, h * CHUNKS, 0, turn)
                act.wait_ge(head_ready, done(h + 1))
                with act.Fori(0, CHUNKS // 2 - 1) as j:
                    step(h, 2 * j, 0, turn + j, True)
                    step(h, 2 * j + 1, 1, turn + j, True)
                step(h, CHUNKS - 2, 0, turn + 3, True)
                step(h, CHUNKS - 1, 1, turn + 3, False)

        @block.vector
        def _(dve):
            ident = res["ident"]
            for s in s_update_done + [s_evac_done[2], s_y_done, s_qk_done, s_masks_done, s_num_done, s_mix_done,
                                      s_end_done]:
                dve.sem_inc(s, 2)
            dve.sem_inc(s_stored, 128)
            for s in [evac_done[2], gateB_done, head_ready, slices_done, dif_done, pw_in_done, cbuf_done, y_done, s2_ready,
                      att_done, num_done, state_done, mix_done]:
                dve.sem_inc(s, 2)
            dve.sem_inc(state_stored, 48)
            dve.sem_inc(conv_stored, 32)
            for b in range(2):
                dve.sem_inc(mix_stored[b], 16)
            chain = Chain(dve, dve_order, 25)
            gateA_chain = Chain(dve, dve_gateA_order, 4)
            gateB_chain = Chain(dve, dve_gateB_order, 3)
            dve.wait_ge(params_loaded, 16 * 2 * (2 * HEADS + 1))

            def gate_a(n, h, b):
                gateA_chain.step(n)
                dve.wait_ge(exp_done[2], done(n + 1))
                chain_ = gateA_chain
                chain_(nc.vector.tensor_scalar(gtmp[:], eA[:, 0:DV], 1.0, None, ALU.add))
                chain_(nc.vector.scalar_tensor_tensor(out=gtmp[:], in0=eA[:, DV:], scalar=1.0, in1=gtmp[:],
                                                      op0=ALU.add, op1=ALU.mult))
                chain_(nc.vector.reciprocal(gtmp[:], gtmp[:]))
                nc.vector.tensor_tensor(gateA[:, b, :], pj[0][:, 0:DV], gtmp[:], ALU.mult).then_inc(evac_done[2], 1)
                dve.wait_ge(evac_done[2], done(n + 1))
                chain_(nc.vector.tensor_tensor(gateA[:, b, :], gateA[:, b, :], gainA[:],
                                               ALU.mult))

            def gate_b(n, h, b):
                dve.wait_ge(evac_done[3], done(n + 1))
                chain_ = gateB_chain
                chain_.step(n)
                chain_(nc.vector.tensor_scalar(gtmp[:], eB[:, 0:DV], 1.0, None, ALU.add))
                chain_(nc.vector.scalar_tensor_tensor(out=gtmp[:], in0=eB[:, DV:], scalar=1.0, in1=gtmp[:],
                                                      op0=ALU.add, op1=ALU.mult))
                chain_(nc.vector.reciprocal(gateB[:, b, :], gtmp[:]))
                chain_.end()
                nc.vector.tensor_tensor(gateB[:, b, :], gateB[:, b, :], gainB[:],
                                        ALU.mult).then_inc(gateB_done, 1)

            def step(h, c, b, turn, ahead):
                n = h * CHUNKS + c
                chain.step(n)
                nc.vector.tensor_scalar(gc[:, b, :], res["gates"][:, bass.ds(c, 1), :]
                                        .rearrange("p a (q g) -> p (a g) q", q=4)[:, bass.ds(h, 1), :]
                                        .rearrange("p a q -> p (a q)"), 1.0, None, ALU.mult).then_inc(slices_done, 1)
                dve.wait_ge(slices_done, done(n + 1))
                dve.wait_ge(m_loaded[b], 48 * turn + 48)
                nc.vector.tensor_copy(refs[:, 0:NSUB], dcy[:, b, SUB // 2 - 1::SUB])
                chain(nc.vector.tensor_copy(refs[:, NSUB:], dcy[:, b, P - 1:P]))
                nc.vector.tensor_tensor(dif[:, 0:NSUB + 1, :], bc(refs[:], 2, P), bc(dcy[:, b, :], 1, NSUB + 1), ALU.subtract)
                chain(nc.vector.tensor_tensor(dif[:, NSUB + 1, :].rearrange("p (i t) -> p i t", i=NSUB),
                                              dcy[:, b, :].rearrange("p (i t) -> p i t", i=NSUB),
                                              bc(refs[:, 0:NSUB], 2, SUB), ALU.subtract))
                nc.vector.tensor_scalar(dif[:], dif[:], TAU * CLAMP, None, ALU.min).then_inc(dif_done, 1)
                nc.vector.tensor_scalar(pw[:], mb[:, b, :], gc[:, b, 0:1], 0.0, ALU.subtract, ALU.max)\
                    .then_inc(pw_in_done, 1)
                dve.wait_ge(t1_done, done(n + 1))
                dve.wait_ge(cbuf_done, done(n))
                nc.vector.tensor_copy(cbuf[:, b, :, CONV - 1:], trB[:].rearrange("p (k t) -> p k t", k=4))
                nc.vector.tensor_copy(cbuf[:, b, :, 0:CONV - 1], cbuf[:, 1 - b, :, P:]).then_inc(cbuf_done, 1)
                dve.wait_ge(dif_exp_done, done(n + 1))
                dve.wait_ge(e0_done, done(n + 1))
                nc.vector.scalar_tensor_tensor(out=qI[:], in0=trA[:, 0:P], scalar=GLA_SCALE, in1=dif[:, NSUB + 1, :],
                                               op0=ALU.mult, op1=ALU.mult)
                nc.vector.scalar_tensor_tensor(out=q0[:], in0=trA[:, 0:P], scalar=GLA_SCALE, in1=e0[:],
                                               op0=ALU.mult, op1=ALU.mult)
                nc.vector.tensor_tensor(kI[:], bc(trA[:, P:2 * P], 1, NSUB + 1), dif[:, 0:NSUB + 1, :], ALU.mult)
                dve.wait_ge(pw_exp_done, done(n + 1))
                nc.vector.tensor_tensor(pw[:], pw[:], res["upper"][:], ALU.mult)
                dve.wait_ge(tap_done, done(n + 1))
                for j in range(1, CONV):
                    for t in range(4):
                        last = nc.vector.scalar_tensor_tensor(
                            out=y[:, t, :], in0=cbuf[:, b, t, j:j + P], scalar=taps[:, t // 2, t % 2, j:j + 1],
                            in1=y[:, t, :], op0=ALU.mult, op1=ALU.add)
                    if j < CONV - 1:
                        chain(last)
                last.then_inc(y_done, 1)
                dve.wait_ge(ey_done, done(n + 1))
                chain(nc.vector.tensor_scalar(ey[:], ey[:], 1.0, None, ALU.add))
                chain(nc.vector.reciprocal(ey[:], ey[:]))
                nc.vector.tensor_tensor(qkT[:, 0:2, :], y[:, 0:2, :], ey[:, 0:2, :], ALU.mult)
                nc.vector.scalar_tensor_tensor(out=qkT[:, 2:4, :], in0=y[:, 2:4, :], scalar=ML_SCALE,
                                               in1=ey[:, 2:4, :], op0=ALU.mult, op1=ALU.mult).then_inc(s2_ready, 1)
                dve.wait_ge(s2_done, done(n + 1))
                for i in range(NSUB):
                    m, lo = (i + 1) * SUB, i * SUB
                    nc.vector.tensor_tensor(attT[0:m, lo:lo + SUB], trA[0:m, 256 + lo:256 + lo + SUB],
                                            res["upper"][0:m, lo:lo + SUB], ALU.mult)
                nc.vector.tensor_tensor(sT[:], trA[:, 384:512], pw[:], ALU.mult).then_inc(att_done, 1)
                if ahead:
                    gate_a(n + 1, h, 1 - b)
                dve.wait_ge(s3_done, done(n + 1))
                chain(nc.vector.tensor_tensor(num[:], pnum[:, 0:DV + 1], inter[:], ALU.add))
                chain(nc.vector.scalar_tensor_tensor(out=den[:, 0:1], in0=num[:, DV:DV + 1], scalar=-1.0,
                                                     in1=num[:, DV:DV + 1], op0=ALU.mult, op1=ALU.max))
                chain(nc.vector.tensor_tensor(den[:, 1:2], den[:, 0:1], gc[:, b, 2:3], ALU.max))
                nc.vector.reciprocal(den[:, 2:3], den[:, 1:2]).then_inc(num_done, 1)
                nc.vector.scalar_tensor_tensor(out=S[:], in0=S[:], scalar=e0[:, P - 1:P], in1=trA[:, 0:DV],
                                               op0=ALU.mult, op1=ALU.add)
                nc.vector.scalar_tensor_tensor(out=C[:, 0, :], in0=C[:, 0, :], scalar=fcb[:, b, :],
                                               in1=pint[:, 0:DV + 1], op0=ALU.mult, op1=ALU.add)
                nc.vector.scalar_tensor_tensor(out=C[:, 1, :], in0=C[:, 1, :], scalar=fcb[:, b, :],
                                               in1=trB[:, 0:DV + 1], op0=ALU.mult, op1=ALU.add).then_inc(state_done, 1)
                dve.wait_ge(squares_done, done(n + 1))
                dve.wait_ge(gateB_done, done(n + 1))
                dve.wait_ge(s4_done, done(n))
                chain(rsqrt_pair(chain, nc.vector, stat, DV))
                chain(nc.vector.tensor_tensor(comb[:], den[:, 2:3], stat[:, 2, 1:2], ALU.mult))
                nc.vector.scalar_tensor_tensor(out=mixA[:], in0=pgla[:, 0:DV], scalar=stat[:, 2, 0:1],
                                               in1=gateA[:, b, :], op0=ALU.mult, op1=ALU.mult)
                chain(nc.vector.scalar_tensor_tensor(out=mix[:], in0=num[:, 0:DV], scalar=comb[:],
                                                     in1=gateB[:, b, :], op0=ALU.mult, op1=ALU.mult))
                nc.vector.tensor_tensor(mix[:], mix[:], mixA[:], ALU.add).then_inc(mix_done, 1)
                chain.end()
                if ahead:
                    gate_b(n + 1, h, 1 - b)

            sample_chain = Chain(dve, dve_sample_order, 37)

            def sample_inputs(h):
                chain = sample_chain
                chain.step(h)
                dve.wait_ge(s_a_done, done(1))
                nc.vector.tensor_scalar(s_a[:], s_a_all[:, bass.ds(h, 1), :].rearrange("p a b -> p (a b)"), 1.0, None,
                                        ALU.mult)
                chain(nc.vector.tensor_scalar(s_gc[:], res["gates_s"][:].rearrange("p (q g) -> p g q", q=4)
                                              [:, bass.ds(h, 1), :].rearrange("p a q -> p (a q)"), 1.0, None,
                                              ALU.mult))
                dve.wait_ge(s_loaded, 160 * h + 160)
                chain(nc.vector.tensor_tensor(s_prod, s_hist[:], s_taps[:, 0:CONV - 1, :], ALU.mult))
                chain(nc.vector.tensor_tensor(s_y, s_prod[:, 0, :], s_taps[:, CONV, :], ALU.add))
                for j in range(1, CONV - 1):
                    chain(nc.vector.tensor_tensor(s_y, s_y, s_prod[:, j, :], ALU.add))
                dve.wait_ge(s_evac_done[1], done(h + 1))
                chain(nc.vector.tensor_tensor(s_prod[:, 0, :], s_bqk[:], s_taps[:, CONV - 1, :], ALU.mult))
                nc.vector.tensor_tensor(s_y, s_y, s_prod[:, 0, :], ALU.add).then_inc(s_y_done, 1)
                dve.wait_ge(s_ey_done, done(h + 1))
                chain(nc.vector.tensor_scalar(s_ey, s_ey, 1.0, None, ALU.add))
                chain(nc.vector.reciprocal(s_ey, s_ey))
                nc.vector.tensor_tensor(s_qk[:, 0:DV], s_y[:, 0:DV], s_ey[:, 0:DV], ALU.mult)
                nc.vector.scalar_tensor_tensor(out=s_qk[:, DV:], in0=s_y[:, DV:], scalar=ML_SCALE, in1=s_ey[:, DV:],
                                               op0=ALU.mult, op1=ALU.mult).then_inc(s_qk_done, 1)
                dve.wait_ge(s_exp_done, done(h + 1))
                chain(nc.vector.tensor_scalar(s_gateB[:], s_eA[:, 0:DV], 1.0, None, ALU.add))
                chain(nc.vector.scalar_tensor_tensor(out=s_gateB[:], in0=s_eA[:, DV:], scalar=1.0, in1=s_gateB[:],
                                                     op0=ALU.add, op1=ALU.mult))
                chain(nc.vector.reciprocal(s_gateB[:], s_gateB[:]))
                nc.vector.tensor_tensor(s_gateA[:], pj[0][0:NS, 0:DV], s_gateB[:], ALU.mult)\
                    .then_inc(s_evac_done[2], 1)
                dve.wait_ge(s_evac_done[2], done(h + 1))
                chain(nc.vector.tensor_tensor(s_gateA[:], s_gateA[:], gainA[0:NS, :], ALU.mult))
                dve.wait_ge(s_evac_done[3], done(h + 1))
                chain(nc.vector.tensor_scalar(s_gateB[:], s_eB[:, 0:DV], 1.0, None, ALU.add))
                chain(nc.vector.scalar_tensor_tensor(out=s_gateB[:], in0=s_eB[:, DV:], scalar=1.0, in1=s_gateB[:],
                                                     op0=ALU.add, op1=ALU.mult))
                chain(nc.vector.reciprocal(s_gateB[:], s_gateB[:]))
                chain(nc.vector.tensor_tensor(s_gateB[:], s_gateB[:], gainB[0:NS, :], ALU.mult))

            def sample_masks(h):
                chain = sample_chain
                dve.wait_ge(s_qk_done, done(h + 1))
                eye = ident[0:NS, 0:NS]
                nc.vector.tensor_tensor(s_km, bc(s_qkv[:, DK:2 * DK], 1, NS), bc(eye, 2, DK), ALU.mult)
                chain(nc.vector.tensor_scalar(s_kw[:], s_qk[:, DV:], s_gc[:, 3:4], None, ALU.mult))
                nc.vector.tensor_tensor(s_kwm[:], bc(s_kw[:], 1, NS), bc(eye, 2, DV), ALU.mult)
                chain(nc.vector.scalar_tensor_tensor(out=s_n[:], in0=s_n[:], scalar=s_gc[:, 1:2], in1=s_kw[:],
                                                     op0=ALU.mult, op1=ALU.add))
                chain(nc.vector.tensor_tensor_reduce(s_qn, s_qk[:, 0:DV], s_n[:], 1.0, 0.0, ALU.mult, ALU.add,
                                                     s_den[:, 3:4]))
                dve.wait_ge(s_qT_done, done(h + 1))
                nc.vector.scalar_tensor_tensor(out=s_qd[:, 0], in0=bc(trA[:, 0:NS], 2, NS), scalar=GLA_SCALE,
                                               in1=res["eye8"][:], op0=ALU.mult, op1=ALU.mult)
                for t in range(2):
                    last = nc.vector.tensor_tensor(s_qd[:, 1 + t], bc(trA[:, (1 + t) * NS:(2 + t) * NS], 2, NS),
                                                   res["eye8"][:], ALU.mult)
                last.then_inc(s_masks_done, 1)

            def sample_update(i, h):
                dve.wait_ge(s_state_loaded, 48 * h + 48)
                dve.wait_ge(s_outer_done[i], done(h + 1))
                for q in range(NS):
                    got = s_banks[q // 2][:, (q % 2) * DV:(q % 2 + 1) * DV]
                    if i == 0:
                        state, f = s_S[:, q, :], s_a[:, q:q + 1]
                    else:
                        tok = (i - 1) * 4 + q // 2
                        state, f = s_C[:, tok, q % 2, :], s_f[:, tok:tok + 1]
                    last = nc.vector.scalar_tensor_tensor(out=state, in0=state, scalar=f, in1=got,
                                                          op0=ALU.mult, op1=ALU.add)
                last.then_inc(s_update_done[i], 1)

            def sample_mix(h):
                chain = sample_chain
                dve.wait_ge(s_out_done, done(h + 1))
                nc.vector.tensor_copy(s_num, pnum[0:NS, 0:DV])
                chain(nc.vector.scalar_tensor_tensor(out=s_den[:, 0:1], in0=s_den[:, 3:4], scalar=-1.0,
                                                     in1=s_den[:, 3:4], op0=ALU.mult, op1=ALU.max))
                chain(nc.vector.tensor_tensor(s_den[:, 1:2], s_den[:, 0:1], s_gc[:, 2:3], ALU.max))
                nc.vector.reciprocal(s_den[:, 2:3], s_den[:, 1:2]).then_inc(s_num_done, 1)
                dve.wait_ge(s_squares_done, done(h + 1))
                dve.wait_ge(s4_done, done(h * CHUNKS))
                chain(rsqrt_pair(chain, nc.vector, s_stat, DV))
                chain(nc.vector.tensor_tensor(s_comb[:], s_den[:, 2:3], s_stat[:, 2, 1:2], ALU.mult))
                nc.vector.scalar_tensor_tensor(out=s_mixA, in0=pgla[0:NS, 0:DV], scalar=s_stat[:, 2, 0:1],
                                               in1=s_gateA[:], op0=ALU.mult, op1=ALU.mult)
                chain(nc.vector.scalar_tensor_tensor(out=s_mix, in0=s_num, scalar=s_comb[:],
                                                     in1=s_gateB[:], op0=ALU.mult, op1=ALU.mult))
                nc.vector.tensor_tensor(s_mix, s_mix, s_mixA, ALU.add).then_inc(s_mix_done, 1)
                dve.wait_ge(s_mT_done, done(h + 1))
                nc.vector.tensor_scalar(res["mixTs"][:, bass.ds(2 * h, 2), :],
                                        trA[:, 0:2 * NS].rearrange("p (k t) -> p k t", k=2), 1.0, None, ALU.mult)\
                    .then_inc(s_end_done, 1)
                chain.end()

            with dve.Fori(0, HEADS) as h:
                turn = h * (CHUNKS // 2)
                dve.wait_ge(state_stored, 48 * h + 48)
                nc.vector.memset(S[:], 0.0)
                nc.vector.memset(C[:], 0.0)
                nc.vector.memset(cbuf[:, 1, :, P:], 0.0)
                for a in range(2):
                    last = nc.vector.tensor_copy(taps[:, a], taps_all[:, a, bass.ds(2 * h, 2), :])
                last.then_inc(head_ready, 1)
                dve.wait_ge(head_ready, done(h + 1))
                sample_inputs(h)
                sample_masks(h)
                sample_update(0, h)
                sample_update(1, h)
                gate_a(h * CHUNKS, h, 0)
                sample_update(2, h)
                gate_b(h * CHUNKS, h, 0)
                sample_mix(h)
                with dve.Fori(0, CHUNKS // 2 - 1) as j:
                    step(h, 2 * j, 0, turn + j, True)
                    step(h, 2 * j + 1, 1, turn + j, True)
                step(h, CHUNKS - 2, 0, turn + 3, True)
                step(h, CHUNKS - 1, 1, turn + 3, False)


RU = 4
RV = 8
RD = 8
PAIRS = PH // 2


def freed(count):
    return count + 10


def peer(nc, io, res):
    with ExitStack() as ctx:
        def sb(name, shape, dt=F32):
            return ctx.enter_context(nc.sbuf_tensor("c_" + name, shape, dt))

        def psum(name, shape):
            return ctx.enter_context(nc.psum_tensor("c_" + name, shape, F32))

        def sem(name):
            return ctx.enter_context(nc.semaphore("c_" + name))

        wout = sb("wout", [P, KT, D])
        wq = sb("wq", [P, KT, PH * 2 * DK])
        subT = sb("subT", [P, 2, NK])
        g2 = sb("g2", [P, D])
        fg = sb("fg", [P, D])
        x2 = sb("x2", [P, 2, D])
        h2 = sb("h2", [P, 2, D])
        mT = sb("mT", [P, KT, P])
        hT = sb("hT", [P, KT, P])
        qs = sb("qs", [P, 2 * DK])
        qT = sb("qT", [P, 2, P])
        ub = sb("ub", [P, RU, D])
        vb = sb("vb", [P, RV, D])
        vacc = sb("vacc", [P, D])
        yt = sb("yt", [P, D])
        diag = sb("diag", [P, RD, P])
        sv = sb("sv", [P, 2, TOPK])
        si = sb("si", [P, 2, TOPK], U32)
        sif = sb("sif", [P, 2, TOPK])
        rest = sb("rest", [P, 2, NK])
        cand = sb("cand", [P, TOPK * TOPK])
        crest = sb("crest", [P, TOPK * TOPK])
        tv = sb("tv", [P, TOPK])
        tp = sb("tp", [P, TOPK], U32)
        pi = sb("pi", [P, 2, TOPK], U32)
        pf = sb("pf", [P, 2, TOPK])
        hot = sb("hot", [P, 2, TOPK, TOPK])
        es = sb("es", [P, 2, TOPK])
        iota_i = sb("iota_i", [P, TOPK], I32)
        iota = sb("iota", [P, TOPK])
        idx = sb("idx", [P, 2, PH, TOPK], U32)
        idx_u = sb("idx_u", [P, 2, TOPK], U32)
        idx_v = sb("idx_v", [P, 2, TOPK], U32)
        tvm = sb("tvm", [P, PH, TOPK])
        gsum = sb("gsum", [P, PH])
        g = sb("g", [P, 2, PH, TOPK])
        a = sb("a", [P, 2, TOPK])
        ga = sb("ga", [P, 2, TOPK])
        w = sb("w", [P, 2, TOPK])
        stat = sb("stat", [P, 4])
        fin = sb("fin", [P, 2])
        fstat = sb("fstat", [P, 4])
        idx_r = sb("idx_r", [P, PH], U32)
        g_r = sb("g_r", [P, PH])
        a_r = sb("a_r", [P, PH])
        w_r = sb("w_r", [P, PH])
        sel = sb("sel", [P, NS])
        w_sel = sb("w_sel", [P, PH, NS])

        po = psum("po", [P, 2, 512])
        pq = psum("pq", [P, 512])
        pqT = psum("pqT", [P, 512])
        psc = [psum(f"psc{i}", [P, 512]) for i in range(2)]
        acc = [psum(f"acc{i}", [P, 512]) for i in range(2)]

        params_loaded = sem("params_loaded")
        wout_loaded = sem("wout_loaded")
        wq_loaded = sem("wq_loaded")
        x_loaded = sem("x_loaded")
        mT_loaded = sem("mT_loaded")
        consts_done = sem("consts_done")
        sub_done = sem("sub_done")
        subT_done = sem("subT_done")
        out_done = sem("out_done")
        x2_done = sem("x2_done")
        h2_done = sem("h2_done")
        hT_done = sem("hT_done")
        hT_copied = sem("hT_copied")
        q_done = sem("q_done")
        q_copied = sem("q_copied")
        qT_done = sem("qT_done")
        qT_copied = sem("qT_copied")
        scores_done = sem("scores_done")
        scores_used = sem("scores_used")
        idx_done = sem("idx_done")
        exp_done = sem("exp_done")
        g_done = sem("g_done")
        staged = sem("staged")
        u_loaded = [sem(f"u_loaded{i}") for i in range(RU)]
        v_loaded = [sem(f"v_loaded{i}") for i in range(RV)]
        u_used = sem("u_used")
        v_dve_used = sem("v_dve_used")
        v_pe_used = sem("v_pe_used")
        gelu_done = sem("gelu_done")
        w_done = sem("w_done")
        diag_done = sem("diag_done")
        zeroed = sem("zeroed")
        residual_done = sem("residual_done")
        acc_done = sem("acc_done")
        squares_done = sem("squares_done")
        y_done = sem("y_done")
        y_stored = sem("y_stored")
        rows_loaded = sem("rows_loaded")
        places_loaded = sem("places_loaded")
        norm_order = sem("norm_order")
        keys_order = sem("keys_order")
        softmax_order = sem("softmax_order")
        final_order = sem("final_order")
        sample_order = sem("sample_order")
        pool_mark = sem("pool_mark")
        dve_mark = sem("dve_mark")
        sp_mark = sem("sp_mark")

        ident = res["ident"]
        block = ctx.enter_context(nc.Block())

        def tiles(eng, body):
            with eng.Fori(0, CHUNKS // 2 - 1) as t:
                body(2 * t, 0, P, P)
                body(2 * t + 1, 1, P, P)
            body(CHUNKS - 2, 0, P, NS)
            body(CHUNKS - 1, 1, NS, None)

        @block.sync
        def _(sp):
            def load_tile(n, b, rows):
                if rows == P:
                    sp.dma_start(x2[:, b, :], io["x_prompt"][bass.ds(n * P, P)]).then_inc(x_loaded, 16)
                    sp.dma_start(mT[:].rearrange("p k t -> p (k t)"),
                                 res["mixT_d"][bass.ds(n, 1)].rearrange("a p k t -> (a p) (k t)")).then_inc(mT_loaded, 16)
                else:
                    sp.dma_start(x2[0:NS, b, :], io["x_sample"]).then_inc(x_loaded, 16)

            load_tile(0, 0, P)
            sp.dma_start(wout[:], io["w_out"].rearrange("(k p) n -> p k n", p=P)).then_inc(wout_loaded, 16)
            for c in range(2):
                sp.dma_start(vb[:, c, 0:DK], io["peer_subkeys"][c]).then_inc(params_loaded, 16)
            sp.dma_start(g2[:], io["norm2_g"].partition_broadcast(P)).then_inc(params_loaded, 16)
            sp.dma_start(fg[:], io["final_g"].partition_broadcast(P)).then_inc(params_loaded, 16)
            for k in range(0, KT, 2):
                sp.dma_start(wq[:, k:k + 2, :], io["peer_wq"][k * P:(k + 2) * P].rearrange("(k p) n -> p k n", p=P))\
                    .then_inc(wq_loaded, 16)
            sp.wait_ge(out_done, done(1))
            load_tile(1, 1, P)

            def spread_sample():
                places = [slice(k * NS, (k + 1) * NS) for k in range(TOPK)]
                sp.wait_ge(h2_done, done(CHUNKS + 1))
                sp.wait_ge(out_done, done(CHUNKS))
                for to in places:
                    sp.dma_start(mT[to].rearrange("p k t -> p (k t)"), h2[0:NS, 0, :]).then_inc(rows_loaded, 16)
                sp.wait_ge(idx_done, done(CHUNKS * PH + PH))
                for k, to in enumerate(places):
                    sp.dma_start(idx_r[to, :], idx[0:NS, 0, :, k]).then_inc(places_loaded, 16)
                sp.wait_ge(g_done, done(CHUNKS + 1))
                for k, to in enumerate(places):
                    sp.dma_start(g_r[to, :], g[0:NS, 0, :, k]).then_inc(rows_loaded, 16)

            def body(i, b, rows_next, rows_after):
                if rows_after is not None:
                    sp.wait_ge(residual_done, done(i + 1))
                    sp.sem_inc(sp_mark, 1)
                    sp.wait_ge(out_done, done(i + 2))
                    sp.sem_inc(sp_mark, 1)
                    load_tile(i + 2, b, rows_after)
                else:
                    spread_sample()
                sp.wait_ge(y_done, done(i + 1))
                sp.sem_inc(sp_mark, 1)
                sp.dma_start(io["y_prompt"][bass.ds(i * P, P)], yt[:]).then_inc(y_stored, 16)

            tiles(sp, body)
            sp.wait_ge(y_done, done(CHUNKS + 1))
            sp.dma_start(io["y_sample"], yt[0:NS, :]).then_inc(y_stored, 16)
            sp.wait_ge(y_stored, 16 * CHUNKS + 32)

        @block.gpsimd
        def _(pool):
            nc.gpsimd.iota(iota_i[:], [[1, TOPK]], base=0, channel_multiplier=0).then_inc(consts_done, 1)
            pool.sem_inc(staged, 2)

            def gather(out, table, at, loaded):
                nc.gpsimd.indirect_dma_start(out=out, out_offset=None, in_=io[table],
                                             in_offset=bass.IndirectOffsetOnAxis(ap=at, axis=0)).then_inc(loaded, 16)

            def gather_u(dh, q, k):
                pool.wait_ge(u_used, freed(dh * TOPK + k - RU + 1))
                pool.sem_inc(pool_mark, 1)
                gather(ub[:, k % RU, :], "peer_u", idx_u[:, q, k:k + 1], u_loaded[k % RU])

            def gather_v(dh, q, k):
                pool.wait_ge(v_pe_used if k % 2 else v_dve_used, freed(dh * (TOPK // 2) + k // 2 - RV // 2 + 1))
                pool.sem_inc(pool_mark, 1)
                gather(vb[:, k % RV, :], "peer_v", idx_v[:, q, k:k + 1], v_loaded[k % RV])

            def stage(to, b, hd, count):
                nc.gpsimd.tensor_copy(to, idx[:, b, bass.ds(hd, 1), :].rearrange("p a k -> p (a k)"))\
                    .then_inc(staged, 1)
                pool.wait_ge(staged, done(count))
                pool.sem_inc(pool_mark, 1)

            def step(dh, q, b, hd, b_next, hd_next):
                if hd_next is not None:
                    pool.wait_ge(idx_done, done(dh + 2))
                    pool.sem_inc(pool_mark, 1)
                    stage(idx_u[:, 1 - q, :], b_next, hd_next, 2 * dh + 2)
                stage(idx_v[:, q, :], b, hd, 2 * dh + (2 if hd_next is None else 3))
                for k in range(TOPK):
                    if hd_next is not None:
                        gather_u(dh + 1, 1 - q, k)
                    gather_v(dh, q, k)

            def body(i, b, rows_next, rows_after):
                dh = i * PH
                with pool.Fori(0, PAIRS - 1) as p:
                    step(dh + 2 * p + 1, 1, b, 2 * p + 1, b, 2 * p + 2)
                    step(dh + 2 * p + 2, 0, b, 2 * p + 2, b, 2 * p + 3)
                if rows_after is None:
                    step(dh + PH - 1, 1, b, PH - 1, None, None)
                else:
                    step(dh + PH - 1, 1, b, PH - 1, 1 - b, 0)
                    step(dh + PH, 0, 1 - b, 0, 1 - b, 1)

            pool.wait_ge(idx_done, done(1))
            stage(idx_u[:, 0, :], 0, 0, 1)
            for k in range(TOPK):
                gather_u(0, 0, k)
            step(0, 0, 0, 0, 0, 1)
            tiles(pool, body)
            pool.wait_ge(places_loaded, 16 * TOPK)
            for h in range(PH):
                pool.wait_ge(u_used, freed(CHUNKS * SLOTS + h - RU + 1))
                pool.sem_inc(pool_mark, 1)
                gather(ub[:, h % RU, :], "peer_u", idx_r[:, h:h + 1], u_loaded[h % RU])
                pool.wait_ge(v_pe_used if h % 2 else v_dve_used, freed(CHUNKS * SLOTS // 2 + h // 2 - RV // 2 + 1))
                pool.sem_inc(pool_mark, 1)
                gather(vb[:, h, :], "peer_v", idx_r[:, h:h + 1], v_loaded[h])

        @block.tensor
        def _(pe):
            for s in [sub_done, out_done, residual_done, hT_done, q_done, qT_done, scores_done, acc_done]:
                pe.sem_inc(s, 2)
            pe.sem_inc(v_pe_used, 10)
            pe.wait_ge(params_loaded, 64)
            for c in range(2):
                last = nc.tensor.transpose(pq[:, c * P:(c + 1) * P], vb[:, c, 0:DK], ident[:])
            last.then_inc(sub_done, 1)

            def out_proj(n, rows, lo, width):
                if rows == P:
                    pe.wait_ge(mT_loaded, 16 * n + 16)
                pe.wait_ge(hT_copied, done(n))
                for k in range(KT):
                    src = mT[:, k, :] if rows == P else res["mixTs"][:, k, :]
                    last = nc.tensor.matmul(po[0:rows].rearrange("p a n -> p (a n)")[:, bass.ds(lo, width)], src,
                                            wout[:, k, bass.ds(lo, width)], start=(k == 0), stop=(k == KT - 1))
                return last

            def transpose_h2(n, b, rows):
                pe.wait_ge(h2_done, done(n + 1))
                for k in range(KT):
                    last = nc.tensor.matmul(po[:, k // 4, (k % 4) * P:(k % 4) * P + rows], h2[0:rows, b, k * P:(k + 1) * P],
                                            ident[0:rows, 0:rows], start=True, stop=True)
                last.then_inc(hT_done, 1)

            def queries(n, hd, rows):
                hh = n * PH + hd
                pe.wait_ge(hT_copied, done(n + 1))
                pe.wait_ge(q_copied, done(hh))
                for k in range(KT):
                    last = nc.tensor.matmul(pq[0:rows, 0:2 * DK], hT[:, k, 0:rows],
                                            wq[:, k, bass.ds(hd * 2 * DK, 2 * DK)], start=(k == 0), stop=(k == KT - 1))
                last.then_inc(q_done, 1)

            def transpose_q(n, hd, rows):
                hh = n * PH + hd
                pe.wait_ge(q_copied, done(hh + 1))
                pe.wait_ge(qT_copied, done(hh))
                for c in range(2):
                    last = nc.tensor.matmul(pqT[:, c * P:c * P + rows], qs[0:rows, c * DK:(c + 1) * DK],
                                            ident[0:rows, 0:rows], start=True, stop=True)
                last.then_inc(qT_done, 1)

            def score(n, hd, q, rows):
                hh = n * PH + hd
                pe.wait_ge(qT_copied, done(hh + 1))
                pe.wait_ge(scores_used, done(hh - 1))
                for c in range(2):
                    last = nc.tensor.matmul(psc[q][0:rows, c * NK:(c + 1) * NK], qT[:, c, 0:rows], subT[:, c, :],
                                            start=True, stop=True)
                last.then_inc(scores_done, 1)

            def add_v(dh, k):
                pe.wait_ge(diag_done, freed(dh * (TOPK // 2) + k // 2 + 1))
                pe.wait_ge(v_loaded[k % RV], 16 * (dh * (TOPK // RV) + k // RV) + 16)
                for half in range(2):
                    last = nc.tensor.matmul(acc[half][:], diag[:, (k // 2) % RD, :],
                                            vb[:, k % RV, half * 512:(half + 1) * 512], start=False, stop=False)
                last.then_inc(v_pe_used, 1)

            def start_acc(i, b, rows):
                pe.wait_ge(y_done, done(i))
                pe.wait_ge(x2_done, done(i + 1))
                for half in range(2):
                    last = nc.tensor.matmul(acc[half][0:rows, :], ident[0:rows, 0:rows],
                                            x2[0:rows, b, half * 512:(half + 1) * 512], start=True, stop=False)
                last.then_inc(residual_done, 1)

            def step(dh, q, n, hd, rows, start=None):
                queries(n, hd, rows)
                if start is not None:
                    start_acc(*start)
                for k in range(1, TOPK, 2):
                    if k == 5:
                        transpose_q(n, hd, rows)
                    if k == 9:
                        score(n, hd, q, rows)
                    add_v(dh, k)

            def body(i, b, rows_next, rows_after):
                dh = i * PH
                quarter = D // PAIRS
                with pe.Fori(0, PAIRS - 1) as p:
                    if rows_after is not None:
                        out_proj(i + 2, rows_after, p * quarter, quarter)
                    step(dh + 2 * p + 1, 1, i + 1, 2 * p + 1, rows_next)
                    step(dh + 2 * p + 2, 0, i + 1, 2 * p + 2, rows_next)
                if rows_after is not None:
                    out_proj(i + 2, rows_after, D - quarter, quarter).then_inc(out_done, 1)
                step(dh + PH - 1, 1, i + 1, PH - 1, rows_next)
                pe.wait_ge(v_dve_used, freed((i + 1) * (SLOTS // 2)))
                for half in range(2):
                    last = nc.tensor.matmul(acc[half][:], ident[:], vacc[:, half * 512:(half + 1) * 512],
                                            start=False, stop=True)
                last.then_inc(acc_done, 1)
                if rows_after is not None:
                    transpose_h2(i + 2, b, rows_after)
                    step(dh + PH, 0, i + 2, 0, rows_after, start=(i + 1, 1 - b, P))

            pe.wait_ge(wout_loaded, 16)
            for half in range(2):
                last = out_proj(0, P, half * 512, 512)
            last.then_inc(out_done, 1)
            transpose_h2(0, 0, P)
            pe.wait_ge(wq_loaded, 16 * KT // 2)
            pe.wait_ge(subT_done, 1)
            queries(0, 0, P)
            for hd in range(PH):
                if hd + 1 < PH:
                    queries(0, hd + 1, P)
                transpose_q(0, hd, P)
                score(0, hd, hd % 2, P)
                if hd == 2:
                    out_proj(1, P, 0, 512)
                if hd == 4:
                    out_proj(1, P, 512, 512).then_inc(out_done, 1)
            transpose_h2(1, 1, P)
            step(0, 0, 1, 0, P, start=(0, 0, P))
            tiles(pe, body)
            start_acc(CHUNKS, 0, NS)
            pe.wait_ge(w_done, done(CHUNKS * PH + 1))
            for h in range(PH):
                pe.wait_ge(v_loaded[h], 16 * (CHUNKS * SLOTS // RV) + 16)
                for half in range(2):
                    last = nc.tensor.matmul(acc[half][0:NS, :], w_sel[:, h, :], vb[:, h, half * 512:(half + 1) * 512],
                                            start=False, stop=(h == PH - 1))
            last.then_inc(acc_done, 1)

        @block.scalar
        def _(act):
            for s in [hT_copied, q_copied, qT_copied, exp_done, gelu_done, squares_done]:
                act.sem_inc(s, 2)
            act.sem_inc(diag_done, 10)
            act.wait_ge(sub_done, done(1))
            nc.scalar.activation(subT[:].rearrange("p c k -> p (c k)"), pq[:, 0:2 * NK], ACT.Copy).then_inc(subT_done, 1)

            def copy_hT(n, rows):
                act.wait_ge(hT_done, done(n + 1))
                act.wait_ge(q_done, done(n * PH))
                for half in range(2):
                    last = nc.scalar.activation(hT[:, half * 4:(half + 1) * 4, 0:rows],
                                                po[:, half, :].rearrange("p (k t) -> p k t", k=4)[:, :, 0:rows], ACT.Copy)
                last.then_inc(hT_copied, 1)

            def copy_q(n, hd, rows):
                hh = n * PH + hd
                act.wait_ge(q_done, done(hh + 1))
                act.wait_ge(qT_done, done(hh))
                nc.scalar.activation(qs[0:rows, :], pq[0:rows, 0:2 * DK], ACT.Copy).then_inc(q_copied, 1)

            def copy_qT(n, hd, rows):
                hh = n * PH + hd
                act.wait_ge(qT_done, done(hh + 1))
                act.wait_ge(scores_done, done(hh))
                nc.scalar.activation(qT[:, :, 0:rows], pqT[:, 0:2 * P].rearrange("p (c t) -> p c t", c=2)[:, :, 0:rows],
                                     ACT.Copy).then_inc(qT_copied, 1)

            def step(dh, q, n, hd, rows):
                act.wait_ge(u_used, freed((dh + 1) * TOPK))
                act.wait_ge(w_done, done(dh - 1))
                nc.scalar.activation(ga[:, q, :], a[:, q, :], ACT.Gelu).then_inc(gelu_done, 1)
                act.wait_ge(w_done, done(dh + 1))
                for k in range(1, TOPK, 2):
                    if k == 5:
                        copy_q(n, hd, rows)
                    if k == 9:
                        copy_qT(n, hd, rows)
                    act.wait_ge(v_pe_used, freed(dh * (TOPK // 2) + k // 2 - RD + 1))
                    nc.scalar.activation(diag[:, (k // 2) % RD, :], ident[:], ACT.Copy, scale=w[:, q, k:k + 1])\
                        .then_inc(diag_done, 1)

            def softmax_exp(n, rows):
                act.wait_ge(idx_done, done(n * PH + PH))
                nc.scalar.activation(tvm[0:rows], tvm[0:rows], ACT.Exp).then_inc(exp_done, 1)

            def squares(i, rows):
                act.wait_ge(acc_done, done(i + 1))
                act.wait_ge(y_stored, 16 * i + 16)
                for half in range(2):
                    last = nc.scalar.activation(yt[0:rows, half * 512:(half + 1) * 512], acc[half][0:rows, :],
                                                ACT.Square, accum_out=fin[0:rows, half:half + 1])
                last.then_inc(squares_done, 1)

            def body(i, b, rows_next, rows_after):
                dh = i * PH
                with act.Fori(0, PAIRS - 1) as p:
                    step(dh + 2 * p + 1, 1, i + 1, 2 * p + 1, rows_next)
                    step(dh + 2 * p + 2, 0, i + 1, 2 * p + 2, rows_next)
                step(dh + PH - 1, 1, i + 1, PH - 1, rows_next)
                softmax_exp(i + 1, rows_next)
                squares(i, P)
                if rows_after is not None:
                    copy_hT(i + 2, rows_after)
                    step(dh + PH, 0, i + 2, 0, rows_after)

            copy_hT(0, P)
            with act.Fori(0, PAIRS) as p:
                for q in range(2):
                    copy_q(0, 2 * p + q, P)
                    copy_qT(0, 2 * p + q, P)
            softmax_exp(0, P)
            copy_hT(1, P)
            step(0, 0, 1, 0, P)
            tiles(act, body)
            act.wait_ge(u_used, freed(CHUNKS * SLOTS + PH))
            nc.scalar.activation(a_r[:], a_r[:], ACT.Gelu).then_inc(gelu_done, 1)
            squares(CHUNKS, NS)

        @block.vector
        def _(dve):
            norm_chain = Chain(dve, norm_order, 12)
            keys_chain = Chain(dve, keys_order, 13, mark=dve_mark)
            softmax_chain = Chain(dve, softmax_order, 2)
            final_chain = Chain(dve, final_order, 12)
            for s in [x2_done, h2_done, scores_used, idx_done, g_done, w_done, zeroed, y_done]:
                dve.sem_inc(s, 2)
            for s in [u_used, v_dve_used]:
                dve.sem_inc(s, 10)
            dve.sem_inc(y_stored, 16)
            dve.wait_ge(consts_done, 1)
            nc.vector.tensor_copy(iota[:], iota_i[:]).then_inc(consts_done, 1)
            nc.vector.tensor_reduce(sel[:], ident[:].rearrange("p (k t) -> p t k", t=NS), AX_X, ALU.add)\
                .then_inc(consts_done, 1)
            dve.wait_ge(consts_done, 3)

            def norm2(n, b, rows):
                chain = norm_chain
                chain.step(n)
                dve.wait_ge(out_done, done(n + 1))
                dve.wait_ge(x_loaded, 16 * n + 16)
                for half in range(2):
                    cols = slice(half * 512, (half + 1) * 512)
                    last = nc.vector.tensor_tensor(x2[0:rows, b, cols], x2[0:rows, b, cols], po[0:rows, half, :], ALU.add)
                last.then_inc(x2_done, 1)
                dve.wait_ge(x2_done, done(n + 1))
                chain(nc.vector.tensor_tensor_reduce(h2[0:rows, b, :], x2[0:rows, b, :], x2[0:rows, b, :], 1.0, 0.0,
                                                     ALU.mult, ALU.add, stat[0:rows, 0:1]))
                chain(rsqrt_mean(chain, nc.vector, stat[0:rows], D))
                nc.vector.scalar_tensor_tensor(out=h2[0:rows, b, :], in0=x2[0:rows, b, :], scalar=stat[0:rows, 2:3],
                                               in1=g2[0:rows, :], op0=ALU.mult, op1=ALU.mult).then_inc(h2_done, 1)
                chain.end()

            def best_keys(n, hd, q, rows):
                hh = n * PH + hd
                chain = keys_chain
                chain.step(hh)
                dve.wait_ge(scores_done, done(hh + 1))
                dve.sem_inc(dve_mark, 1)
                sides = [(psc[q][0:rows, c * NK:(c + 1) * NK], sv[0:rows, c, :], si[0:rows, c, :], rest[0:rows, c, :])
                         for c in range(2)]
                for s, v, _, _ in sides:
                    last = nc.vector.max(out=v[:, 0:8], in_=s)
                chain(last)
                for s, v, i, r in sides:
                    nc.vector.max_index(out=i[:, 0:8], in_max=v[:, 0:8], in_values=s)
                    last = nc.vector.match_replace(out=r, in_to_replace=v[:, 0:8], in_values=s, imm_value=NEG)
                last.then_inc(scores_used, 1)
                dve.wait_ge(scores_used, done(hh + 1))
                dve.sem_inc(dve_mark, 1)
                for _, v, _, r in sides:
                    last = nc.vector.max(out=v[:, 8:16], in_=r)
                chain(last)
                for _, v, i, r in sides:
                    last = nc.vector.max_index(out=i[:, 8:16], in_max=v[:, 8:16], in_values=r)
                chain(last)

            def best_sums(n, hd, rows):
                chain = keys_chain
                c_in, c_out, t_v, t_p = cand[0:rows], crest[0:rows], tv[0:rows], tp[0:rows]
                nc.vector.tensor_copy(sif[0:rows], si[0:rows])
                chain(nc.vector.tensor_tensor(c_in.rearrange("p (a b) -> p a b", a=TOPK), bc(sv[0:rows, 0, :], 2, TOPK),
                                              bc(sv[0:rows, 1, :], 1, TOPK), ALU.add))
                chain(nc.vector.max(out=t_v[:, 0:8], in_=c_in))
                nc.vector.max_index(out=t_p[:, 0:8], in_max=t_v[:, 0:8], in_values=c_in)
                chain(nc.vector.match_replace(out=c_out, in_to_replace=t_v[:, 0:8], in_values=c_in, imm_value=NEG))
                chain(nc.vector.max(out=t_v[:, 8:16], in_=c_out))
                chain(nc.vector.max_index(out=t_p[:, 8:16], in_max=t_v[:, 8:16], in_values=c_out))

            def pick(n, hd, b, rows):
                chain = keys_chain
                t_v, t_p = tv[0:rows], tp[0:rows]
                nc.vector.tensor_scalar(tvm[0:rows, bass.ds(hd, 1), :].rearrange("p a k -> p (a k)"), t_v, t_v[:, 0:1],
                                        None, ALU.subtract)
                nc.vector.tensor_scalar(pi[0:rows, 0, :], t_p, 4, None, ALU.logical_shift_right)
                chain(nc.vector.tensor_scalar(pi[0:rows, 1, :], t_p, 15, None, ALU.bitwise_and))
                chain(nc.vector.tensor_copy(pf[0:rows], pi[0:rows]))
                for c in range(2):
                    last = nc.vector.tensor_tensor(hot[0:rows, c], bc(pf[0:rows, c, :], 2, TOPK),
                                                   bc(iota[0:rows, :], 1, TOPK), ALU.is_equal)
                chain(last)
                for c in range(2):
                    last = nc.vector.tensor_tensor(hot[0:rows, c], hot[0:rows, c], bc(sif[0:rows, c, :], 1, TOPK), ALU.mult)
                chain(last)
                chain(nc.vector.tensor_reduce(es[0:rows], hot[0:rows], AX_X, ALU.add))
                nc.vector.scalar_tensor_tensor(out=idx[0:rows, b, bass.ds(hd, 1), :].rearrange("p a k -> p (a k)"),
                                               in0=es[0:rows, 0, :], scalar=float(NK), in1=es[0:rows, 1, :],
                                               op0=ALU.mult, op1=ALU.add).then_inc(idx_done, 1)
                chain.end()

            def softmax(n, b, rows):
                chain = softmax_chain
                chain.step(n)
                dve.wait_ge(exp_done, done(n + 1))
                chain(nc.vector.tensor_reduce(gsum[0:rows, :], tvm[0:rows], AX_X, ALU.add))
                chain(nc.vector.reciprocal(gsum[0:rows, :], gsum[0:rows, :]))
                chain.end()
                nc.vector.tensor_tensor(g[0:rows, b], tvm[0:rows], bc(gsum[0:rows, :], 2, TOPK), ALU.mult)\
                    .then_inc(g_done, 1)

            def dot_u(dh, q, b, k):
                dve.wait_ge(u_loaded[k % RU], 16 * (dh * (TOPK // RU) + k // RU) + 16)
                nc.vector.tensor_tensor_reduce(ub[:, k % RU, :], ub[:, k % RU, :], h2[:, b, :], 1.0, 0.0, ALU.mult,
                                               ALU.add, a[:, q, k:k + 1]).then_inc(u_used, 1)

            def weigh(dh, q, b, hd):
                dve.wait_ge(diag_done, freed((dh - 1) * (TOPK // 2)))
                dve.wait_ge(gelu_done, done(dh + 1))
                nc.vector.tensor_tensor(w[:, q, :], ga[:, q, :], g[:, b, bass.ds(hd, 1), :].rearrange("p a k -> p (a k)"),
                                        ALU.mult).then_inc(w_done, 1)
                dve.wait_ge(w_done, done(dh + 1))

            def add_v(dh, q, k):
                dve.wait_ge(v_loaded[k % RV], 16 * (dh * (TOPK // RV) + k // RV) + 16)
                dve.wait_ge(v_dve_used, freed(dh * (TOPK // 2) + k // 2))
                nc.vector.scalar_tensor_tensor(out=vacc[:], in0=vb[:, k % RV, :], scalar=w[:, q, k:k + 1], in1=vacc[:],
                                               op0=ALU.mult, op1=ALU.add).then_inc(v_dve_used, 1)

            def final_norm(i, rows):
                chain = final_chain
                chain.step(i)
                dve.wait_ge(squares_done, done(i + 1))
                chain(nc.vector.tensor_tensor(fstat[0:rows, 0:1], fin[0:rows, 0:1], fin[0:rows, 1:2], ALU.add))
                chain(rsqrt_mean(chain, nc.vector, fstat[0:rows], D))
                chain.end()
                for half in range(2):
                    cols = slice(half * 512, (half + 1) * 512)
                    last = nc.vector.scalar_tensor_tensor(out=yt[0:rows, cols], in0=acc[half][0:rows, :],
                                                          scalar=fstat[0:rows, 2:3], in1=fg[0:rows, cols],
                                                          op0=ALU.mult, op1=ALU.mult)
                last.then_inc(y_done, 1)

            def find(n, hd, q, b, rows):
                best_keys(n, hd, q, rows)
                best_sums(n, hd, rows)
                pick(n, hd, b, rows)

            def step(dh, q, b, hd, b_u, n, hd_n, b_n, rows, start=None, end=None):
                at = 1 if start is None else 3
                todo = list(range(0, TOPK, 2))
                for k in range(TOPK):
                    if b_u is not None:
                        dot_u(dh + 1, 1 - q, b_u, k)
                    if k == at:
                        if start is not None:
                            start()
                        weigh(dh, q, b, hd)
                    while k >= at and todo and (todo[0] < k or k == TOPK - 1):
                        add_v(dh, q, todo.pop(0))
                    if k == 8:
                        best_keys(n, hd_n, q, rows)
                    if k == 11:
                        best_sums(n, hd_n, rows)
                    if k == 14:
                        pick(n, hd_n, b_n, rows)
                    if k == 14 and end is not None:
                        end()

            def zero(i):
                dve.wait_ge(acc_done, done(i))
                nc.vector.memset(vacc[:], 0.0).then_inc(zeroed, 1)
                dve.wait_ge(zeroed, done(i + 1))

            def body(i, b, rows_next, rows_after):
                dh = i * PH
                dve.wait_ge(staged, done(dh * 2 + 3))
                dve.sem_inc(dve_mark, 1)
                with dve.Fori(0, PAIRS - 1) as p:
                    dve.wait_ge(gelu_done, done(dh + 2 * p + 1))
                    step(dh + 2 * p + 1, 1, b, 2 * p + 1, b, i + 1, 2 * p + 1, 1 - b, rows_next)
                    step(dh + 2 * p + 2, 0, b, 2 * p + 2, b, i + 1, 2 * p + 2, 1 - b, rows_next)

                def end_tile():
                    softmax(i + 1, 1 - b, rows_next)
                    zero(i + 1)
                    final_norm(i, P)

                if rows_after is None:
                    step(dh + PH - 1, 1, b, PH - 1, None, i + 1, PH - 1, 1 - b, rows_next)
                    softmax(i + 1, 1 - b, rows_next)
                    final_norm(i, P)
                else:
                    step(dh + PH - 1, 1, b, PH - 1, 1 - b, i + 1, PH - 1, 1 - b, rows_next,
                         end=lambda: norm2(i + 2, b, rows_after))
                    step(dh + PH, 0, 1 - b, 0, 1 - b, i + 2, 0, b, rows_after, start=end_tile)

            dve.wait_ge(params_loaded, 64)
            norm2(0, 0, P)
            for hd in range(PH):
                find(0, hd, hd % 2, 0, P)
                if hd == 5:
                    norm2(1, 1, P)
                if hd >= PH // 2:
                    for k in range(4 * hd - 4 * PAIRS, 4 * hd - 4 * PAIRS + 4):
                        dot_u(0, 0, 0, k)
            softmax(0, 0, P)
            step(0, 0, 0, 0, 0, 1, 0, 1, P, start=lambda: zero(0))
            tiles(dve, body)
            dve.wait_ge(rows_loaded, 32 * TOPK)
            for h in range(PH):
                dve.wait_ge(u_loaded[h % RU], 16 * (CHUNKS * SLOTS // RU + h // RU) + 16)
                nc.vector.tensor_tensor_reduce(ub[:, h % RU, :], ub[:, h % RU, :], mT[:].rearrange("p k t -> p (k t)"),
                                               1.0, 0.0, ALU.mult, ALU.add, a_r[:, h:h + 1]).then_inc(u_used, 1)
            dve.wait_ge(gelu_done, done(CHUNKS * PH + 1))
            nc.vector.tensor_tensor(w_r[:], a_r[:], g_r[:], ALU.mult).then_inc(sample_order, 1)
            dve.wait_ge(sample_order, 1)
            nc.vector.tensor_tensor(w_sel[:], bc(w_r[:], 2, NS), bc(sel[:], 1, PH), ALU.mult).then_inc(w_done, 1)
            final_norm(CHUNKS, NS)


def build(nc, io):
    with ExitStack() as ctx:
        ctx.enter_context(nc.allow_non_contiguous_dma(reason="small vectors laid over partitions"))

        def sb(name, shape, dt=F32):
            return ctx.enter_context(nc.sbuf_tensor(name, shape, dt))

        def dram(name, shape):
            return nc.dram_tensor(name, shape, F32, kind="Internal").ap()

        res = {
            "ident": sb("ident", [P, P]),
            "upper": sb("upper", [P, P]),
            "eye8": sb("eye8", [P, NS, NS]),
            "hTs": sb("hTs", [P, KT, NS]),
            "hT_d": dram("hT_d", [CHUNKS, P, KT * P]),
            "decay_d": dram("decay_d", [CHUNKS, P, HEADS * P]),
            "m_d": dram("m_d", [HEADS, T]),
            "fc_d": dram("fc_d", [HEADS, CHUNKS]),
            "fs_d": dram("fs_d", [HEADS, NS]),
            "mixT_d": dram("mixT_d", [CHUNKS, P, KT, P]),
            "mixTs": sb("mixTs", [P, KT, NS]),
        }
        with ExitStack() as gates:
            def gb(name, shape):
                return gates.enter_context(nc.sbuf_tensor(name, shape, F32))

            res["gates"] = gb("gates", [P, CHUNKS, 4 * HEADS])
            res["gates_s"] = gb("gates_s", [NS, 4 * HEADS])
            res["lsig_s"] = gb("lsig_s", [P, HEADS, NS])
            norm1_and_gates(nc, io, res)
            mixer(nc, io, res)
        peer(nc, io, res)


_INS = ["x_prompt", "x_sample", "state_gla", "state_mlstm_c", "state_mlstm_n", "state_mlstm_m", "state_conv",
        "norm1_g", "w_in", "gla_w2", "gla_b2", "gla_norm_g", "conv_w", "conv_b", "ml_i_b", "ml_f_b", "ml_norm_g",
        "w_out", "norm2_g", "peer_wq", "peer_subkeys", "peer_u", "peer_v", "final_g"]
_OUTS = {"y_prompt": (T, D), "y_sample": (NS, D), "p_gla": (HEADS, DK, DV), "p_c": (HEADS, DV, DV),
         "p_n": (HEADS, DV), "p_m": (HEADS,), "p_conv": (CONV - 1, 2 * MLW), "s_gla": (NS, HEADS, DK, DV),
         "s_c": (NS, HEADS, DV, DV), "s_n": (NS, HEADS, DV), "s_m": (NS, HEADS), "s_conv": (NS, CONV - 1, 2 * MLW)}
_SHAPES = {"y_prompt": (1, T, D), "y_sample": (NS, 1, D)}


def kernel(**inputs):
    import numpy as _np
    import concourse.bacc as _bacc
    from concourse import mybir as _mybir
    from concourse.bass_utils import run_bass_kernel_spmd as _run

    nc = _bacc.Bacc("TRN2", target_bir_lowering=False, num_devices=1)
    arrays, io = {}, {}
    for name in _INS:
        a = _np.ascontiguousarray(inputs[name])
        a = a.reshape([n for n in a.shape if n != 1])
        arrays[f"in_{name}"] = a
        io[name] = nc.dram_tensor(f"in_{name}", a.shape, _mybir.dt.from_np(a.dtype), kind="ExternalInput").ap()
    for name, shape in _OUTS.items():
        io[name] = nc.dram_tensor(f"out_{name}", shape, _mybir.dt.float32, kind="ExternalOutput").ap()
    build(nc, io)
    r = _run(nc, [arrays], core_ids=[0])
    return tuple(r.results[0][f"out_{name}"].reshape(_SHAPES.get(name, (1,) + (shape if name[0] == "s" else (1,) + shape)))
                 for name, shape in _OUTS.items())
```
